# Optimizing a Trainium2 kernel written in Bass

```python
import jax, jax.numpy as jnp
from jax import lax
import numpy as np

D_MODEL = 1024
BATCH = 1
SEQ = 512
DEPTH = 1

CHUNK = 64
N_META = 16
HEAD_DIM = 64
N_Q_HEADS = 8
N_KV_HEADS = 2
Q_PER_KV = N_Q_HEADS // N_KV_HEADS
ATTN_WIDTH = N_Q_HEADS * HEAD_DIM
KV_WIDTH = N_KV_HEADS * HEAD_DIM
WINDOW = 128
WINDOW_CHUNKS = WINDOW // CHUNK
LRU_WIDTH = D_MODEL // 2
LRU_BLOCKS = 8
LRU_BLOCK = LRU_WIDTH // LRU_BLOCKS
CONV_WIDTH = 4
LRU_C = 8.0
MIX_WIDTH = ATTN_WIDTH + LRU_WIDTH
IN_WIDTH = ATTN_WIDTH + 2 * KV_WIDTH + 2 * LRU_WIDTH
D_FF = 2816
EPS = 1e-6
ATTN_SCALE = HEAD_DIM ** -0.5
NEG_INF = -1e30

kernel_name = "hymba_rglru_swa_sink_macaron"

def rms_norm(x, g):
    xf = x.astype(jnp.float32)
    y = xf * lax.rsqrt(jnp.mean(xf * xf, axis=-1, keepdims=True) + EPS)
    return (y * g.astype(jnp.float32)).astype(x.dtype)

def swiglu(x, w_gate, w_up, w_down):
    return (jax.nn.silu(x @ w_gate) * (x @ w_up)) @ w_down

def sink_attention(q, k, v, valid, sinks):
    logits = jnp.einsum('bnqhgd,bnkhd->bhgnqk', q, k,
                        preferred_element_type=jnp.float32) * ATTN_SCALE
    logits = jnp.where(valid, logits, NEG_INF)
    s = sinks.astype(jnp.float32)[None, :, :, None, None, None]
    m = jnp.maximum(jnp.max(logits, axis=-1, keepdims=True), s)
    p = jnp.exp(logits - m)
    w = p / (jnp.sum(p, axis=-1, keepdims=True) + jnp.exp(s - m))
    return jnp.einsum('bhgnqk,bnkhd->bnqhgd', w.astype(v.dtype), v)

def windowed_chunk_attention(q, k, v, sinks):
    B, L = q.shape[0], q.shape[1]
    n_chunks = (L - N_META) // CHUNK
    out_meta = sink_attention(q[:, None, :N_META], k[:, None, :N_META], v[:, None, :N_META],
                              jnp.ones((1, 1, N_META), dtype=bool), sinks)
    out_meta = out_meta.reshape(B, N_META, ATTN_WIDTH)
    q_r = q[:, N_META:].reshape(B, n_chunks, CHUNK, N_KV_HEADS, Q_PER_KV, HEAD_DIM)
    k_r = k[:, N_META:].reshape(B, n_chunks, CHUNK, N_KV_HEADS, HEAD_DIM)
    v_r = v[:, N_META:].reshape(B, n_chunks, CHUNK, N_KV_HEADS, HEAD_DIM)
    k_meta = jnp.broadcast_to(k[:, None, :N_META], (B, n_chunks, N_META, N_KV_HEADS, HEAD_DIM))
    v_meta = jnp.broadcast_to(v[:, None, :N_META], (B, n_chunks, N_META, N_KV_HEADS, HEAD_DIM))
    chunk_ids = jnp.arange(n_chunks)[:, None]
    k_parts, v_parts = [k_meta], [v_meta]
    masks = [jnp.ones((n_chunks, N_META), dtype=bool)]
    for d in range(WINDOW_CHUNKS - 1, 0, -1):
        pad = ((0, 0), (d, 0), (0, 0), (0, 0), (0, 0))
        k_parts.append(jnp.pad(k_r[:, :n_chunks - d], pad))
        v_parts.append(jnp.pad(v_r[:, :n_chunks - d], pad))
        masks.append(jnp.broadcast_to(chunk_ids >= d, (n_chunks, CHUNK)))
    k_parts.append(k_r)
    v_parts.append(v_r)
    masks.append(jnp.ones((n_chunks, CHUNK), dtype=bool))
    keys = jnp.concatenate(k_parts, axis=2)
    vals = jnp.concatenate(v_parts, axis=2)
    valid = jnp.concatenate(masks, axis=-1)[:, None, :]
    out_real = sink_attention(q_r, keys, vals, valid, sinks)
    out_real = out_real.reshape(B, n_chunks * CHUNK, ATTN_WIDTH)
    return jnp.concatenate([out_meta, out_real], axis=1)

def causal_depthwise_conv(x, w, b):
    y = lax.conv_general_dilated(x, w[:, None, :].astype(x.dtype), window_strides=(1,),
                                 padding=[(CONV_WIDTH - 1, 0)],
                                 dimension_numbers=('NWC', 'WIO', 'NWC'),
                                 feature_group_count=x.shape[-1])
    return y + b

def rg_lru(x, w_a, b_a, w_x, b_x, lam):
    B, L, C = x.shape
    xb = x.reshape(B, L, LRU_BLOCKS, LRU_BLOCK)
    r = jax.nn.sigmoid(jnp.einsum('blhi,hij->blhj', xb, w_a) + b_a).reshape(B, L, C)
    i = jax.nn.sigmoid(jnp.einsum('blhi,hij->blhj', xb, w_x) + b_x).reshape(B, L, C)
    log_a = -LRU_C * r.astype(jnp.float32) * jax.nn.softplus(-lam.astype(jnp.float32))
    a = jnp.exp(log_a)
    u = jnp.sqrt(-jnp.expm1(2.0 * log_a)) * (i * x).astype(jnp.float32)

    def combine(left, right):
        a1, b1 = left
        a2, b2 = right
        return a1 * a2, a2 * b1 + b2

    _, h = lax.associative_scan(combine, (a, u), axis=1)
    return h.astype(x.dtype)

def hybrid_mixer(h, w_in, sinks, conv_w, conv_b, lru_wa, lru_ba, lru_wx, lru_bx,
                 lru_lambda, attn_out_norm, lru_out_norm, w_out):
    B, L, _ = h.shape
    proj = h @ w_in
    s1 = ATTN_WIDTH
    s2 = s1 + KV_WIDTH
    s3 = s2 + KV_WIDTH
    s4 = s3 + LRU_WIDTH
    q, k, v, x_lru, gate = jnp.split(proj, [s1, s2, s3, s4], axis=-1)
    q = q.reshape(B, L, N_KV_HEADS, Q_PER_KV, HEAD_DIM)
    k = k.reshape(B, L, N_KV_HEADS, HEAD_DIM)
    v = v.reshape(B, L, N_KV_HEADS, HEAD_DIM)
    y_attn = windowed_chunk_attention(q, k, v, sinks.reshape(N_KV_HEADS, Q_PER_KV))
    x_lru = causal_depthwise_conv(x_lru, conv_w, conv_b)
    y_lru = rg_lru(x_lru, lru_wa, lru_ba, lru_wx, lru_bx, lru_lambda) * jax.nn.gelu(gate)
    y = jnp.concatenate([rms_norm(y_attn, attn_out_norm), rms_norm(y_lru, lru_out_norm)], axis=-1)
    return y @ w_out

def setup_inputs(seed: int = 0) -> dict:
    key = jax.random.key(seed)
    ks = jax.random.split(key, 26)
    f32 = jnp.float32

    def nrm(k, shape, scale):
        return jax.random.normal(k, shape, f32) * scale

    def gain(k, shape):
        return 1.0 + 0.05 * jax.random.normal(k, shape, f32)

    a0 = jax.random.uniform(ks[14], (DEPTH, LRU_WIDTH), f32, minval=0.9, maxval=0.999)
    sig = a0 ** (1.0 / LRU_C)
    lru_lambda = jnp.log(sig) - jnp.log1p(-sig)
    return {
        "x": nrm(ks[0], (BATCH, SEQ, D_MODEL), 1.0),
        "meta_tokens": nrm(ks[1], (N_META, D_MODEL), 1.0),
        "ffn1_norm": gain(ks[2], (DEPTH, D_MODEL)),
        "ffn1_w_gate": nrm(ks[3], (DEPTH, D_MODEL, D_FF), D_MODEL ** -0.5),
        "ffn1_w_up": nrm(ks[4], (DEPTH, D_MODEL, D_FF), D_MODEL ** -0.5),
        "ffn1_w_down": nrm(ks[5], (DEPTH, D_FF, D_MODEL), D_FF ** -0.5),
        "mix_norm": gain(ks[6], (DEPTH, D_MODEL)),
        "w_in": nrm(ks[7], (DEPTH, D_MODEL, IN_WIDTH), D_MODEL ** -0.5),
        "attn_sinks": nrm(ks[8], (DEPTH, N_Q_HEADS), 1.0),
        "conv_w": nrm(ks[9], (DEPTH, CONV_WIDTH, LRU_WIDTH), CONV_WIDTH ** -0.5),
        "conv_b": nrm(ks[10], (DEPTH, LRU_WIDTH), 0.02),
        "lru_wa": nrm(ks[11], (DEPTH, LRU_BLOCKS, LRU_BLOCK, LRU_BLOCK), LRU_BLOCK ** -0.5),
        "lru_ba": nrm(ks[12], (DEPTH, LRU_BLOCKS, LRU_BLOCK), 0.02),
        "lru_wx": nrm(ks[13], (DEPTH, LRU_BLOCKS, LRU_BLOCK, LRU_BLOCK), LRU_BLOCK ** -0.5),
        "lru_bx": nrm(ks[15], (DEPTH, LRU_BLOCKS, LRU_BLOCK), 0.02),
        "lru_lambda": lru_lambda,
        "attn_out_norm": gain(ks[16], (DEPTH, ATTN_WIDTH)),
        "lru_out_norm": gain(ks[17], (DEPTH, LRU_WIDTH)),
        "w_out": nrm(ks[18], (DEPTH, MIX_WIDTH, D_MODEL), MIX_WIDTH ** -0.5),
        "ffn2_norm": gain(ks[19], (DEPTH, D_MODEL)),
        "ffn2_w_gate": nrm(ks[20], (DEPTH, D_MODEL, D_FF), D_MODEL ** -0.5),
        "ffn2_w_up": nrm(ks[21], (DEPTH, D_MODEL, D_FF), D_MODEL ** -0.5),
        "ffn2_w_down": nrm(ks[22], (DEPTH, D_FF, D_MODEL), D_FF ** -0.5),
        "final_norm": gain(ks[23], (D_MODEL,)),
    }

def reference(x, meta_tokens, ffn1_norm, ffn1_w_gate, ffn1_w_up, ffn1_w_down, mix_norm,
              w_in, attn_sinks, conv_w, conv_b, lru_wa, lru_ba, lru_wx, lru_bx, lru_lambda,
              attn_out_norm, lru_out_norm, w_out, ffn2_norm, ffn2_w_gate, ffn2_w_up,
              ffn2_w_down, final_norm):
    B = x.shape[0]
    meta = jnp.broadcast_to(meta_tokens[None].astype(x.dtype), (B, N_META, D_MODEL))
    h = jnp.concatenate([meta, x], axis=1)
    for l in range(DEPTH):
        h = h + 0.5 * swiglu(rms_norm(h, ffn1_norm[l]), ffn1_w_gate[l], ffn1_w_up[l], ffn1_w_down[l])
        h = h + hybrid_mixer(rms_norm(h, mix_norm[l]), w_in[l], attn_sinks[l], conv_w[l], conv_b[l],
                             lru_wa[l], lru_ba[l], lru_wx[l], lru_bx[l], lru_lambda[l],
                             attn_out_norm[l], lru_out_norm[l], w_out[l])
        h = h + 0.5 * swiglu(rms_norm(h, ffn2_norm[l]), ffn2_w_gate[l], ffn2_w_up[l], ffn2_w_down[l])
    h = rms_norm(h, final_norm)
    return h[:, N_META:]


_drawn_inputs = setup_inputs


def setup_inputs(seed=0):
    import zlib

    import numpy as np

    out = dict(_drawn_inputs(seed))
    spreads = {}
    factors = {'attn_sinks': 8.0, 'lru_ba': 8.0, 'lru_bx': 8.0, 'ffn2_norm': 3.917}
    for name, (base, spread) in spreads.items():
        noise = np.random.default_rng([zlib.crc32(name.encode()), seed]).standard_normal(out[name].shape)
        drawn = base * np.exp(spread * noise) if base else spread * noise
        out[name] = __import__('jax').numpy.asarray(drawn.astype(out[name].dtype))
    for name, factor in factors.items():
        out[name] = (out[name] * factor).astype(out[name].dtype)
    return out
```

```python
import math
from contextlib import ExitStack

import concourse.bass as bass
from concourse import mybir

F32 = mybir.dt.float32
F32R = mybir.dt.float32r
ALU = mybir.AluOpType
ACT = mybir.ActivationFunctionType
AX_X = mybir.AxisListType.X

P = 128
D_MODEL, SEQ, N_META, D_FF = 1024, 512, 16, 2816
CHUNK, HEAD_DIM, LRU_WIDTH, CONV_WIDTH = 64, 64, 512, 4
EPS, LRU_C = 1e-6, 8.0
ATTN_SCALE = HEAD_DIM ** -0.5
L = N_META + SEQ
KD = D_MODEL // P
J = D_FF // P
HJ = J // 2
NB = LRU_WIDTH // P
NC = SEQ // CHUNK
KEYS = N_META + 2 * CHUNK
ATTN_WIDTH = NB * P
SLOTS, RAW = 4, 2

U_GU = (0, 82)
U_DOWN = (44, 126)
U_IN, U_OUT, UNITS = 60, 74, 142
O_GU = (0, 82)
O_DOWN = (44, 126)
O_IN, O_GATE, O_BRANCH, O_OUT = 52, 62, 70, 74

ALL = [(0, 0, L // 2), (1, L // 2, L // 2)]
REAL = [(0, N_META, SEQ)]

VEC = {}
_at = 0
for _name, _n in (("ffn1", KD), ("mix", KD), ("ffn2", KD), ("final", KD), ("attn", NB), ("lru", NB),
                  ("conv_w", CONV_WIDTH * NB), ("conv_b", NB), ("ba", NB), ("bx", NB), ("lam", NB), ("sink", NB)):
    VEC[_name] = _at
    _at += _n
NVEC = _at


def keys(c):
    return KEYS if c else KEYS - CHUNK


def build_layer(nc, x_t, ffn1_gu, ffn1_down, w_in, w_out, ffn2_gu, ffn2_down, gate_w, vecs, out_t):
    with ExitStack() as ctx:
        def sb(name, shape, dt=F32, where=ctx):
            return where.enter_context(nc.sbuf_tensor(name, shape, dt))

        def sem(name):
            return ctx.enter_context(nc.semaphore(name))

        h = sb("h", [P, KD, L])
        xg_head = sb("xg_head", [P, KD, L], F32R)
        xg_tail = sb("xg_tail", [P, KD, L], F32R)
        w_raw = sb("w_raw", [P, RAW, HJ * P])
        w_head = sb("w_head", [P, SLOTS, HJ * P], F32R)
        w_tail = sb("w_tail", [P, SLOTS, HJ * P], F32R)
        rstd = sb("rstd", [P, L])
        square = sb("square", [P, L])
        sum_sq = sb("sum_sq", [P, L])
        ones = sb("ones", [P, P])
        vec = sb("vec", [P, NVEC])
        eps = sb("eps", [P, 1])

        with ExitStack() as ffn:
            hid_head = sb("hid_head", [P, J, L], F32R, ffn)
            hid_tail = sb("hid_tail", [P, J, L], F32R, ffn)
            gate_s = sb("gate_s", [P, L], F32, ffn)
            up_s = sb("up_s", [P, L], F32, ffn)
        with ExitStack() as early:
            q_t = sb("q_t", [P, NB, SEQ], F32, early)
            k_win = sb("k_win", [P, NC, KEYS], F32, early)
        ya_head = sb("ya_head", [P, NB, SEQ], F32R)
        ya_tail = sb("ya_tail", [P, NB, SEQ], F32R)
        with ExitStack() as early:
            k_t = sb("k_t", [P, L], F32, early)
            v_t = sb("v_t", [P, L], F32, early)
        one_m_a2 = sb("one_m_a2", [P, NB, L])
        with ExitStack() as early:
            p_t = sb("p_t", [P, NB * P], F32, early)
            p_t_meta = sb("p_t_meta", [N_META, NB * P], F32, early)
        y_scaled = sb("y_scaled", [P, 2, SEQ])
        with ExitStack() as early:
            gelu = sb("gelu", [P, NB, SEQ], F32, early)
        yl_tail = sb("yl_tail", [P, NB, SEQ], F32R)
        yl_head = sb("yl_head", [P, NB, SEQ], F32R)
        v_win = sb("v_win", [P, NC, P])
        v_meta = sb("v_meta", [N_META, P])
        prob = sb("prob", [P, NB, KEYS])
        y_attn = sb("y_attn", [P, NB, SEQ])
        x_pad = sb("x_pad", [P, CONV_WIDTH - 1 + L])
        xc = sb("xc", [P, NB, L])
        r_a = sb("r_a", [P, NB, L])
        i_u = sb("i_u", [P, NB, L])
        a_sq = sb("a_sq", [P, L])
        gate_bd = sb("gate_bd", [P, 2, NB, P])
        ident = sb("ident", [P, P])
        small = sb("small", [P, 16, NB])
        rstd_attn = i_u[:, 0, 0:SEQ]

        ps = [ctx.enter_context(nc.psum_tensor(f"ps{i}", [P, 2, 512], F32)) for i in range(4)]
        pair = ps[0:2]
        ps_c, ps_d = ps[2], ps[3]

        x_landed = [sem(f"x_landed{k}") for k in range(KD)]
        vec_landed, bd_landed = sem("vec_landed"), sem("bd_landed")
        w_landed = [sem(f"w_landed{r}") for r in range(RAW)]
        head_made, tail_made = sem("head_made"), sem("tail_made")
        units_done = sem("units_done")
        pair_read = [sem("pair_read0"), sem("pair_read1")]
        const_made, mixer_const = sem("const_made"), sem("mixer_const")
        h_ready, xg_head_made, xg_tail_made = sem("h_ready"), sem("xg_head_made"), sem("xg_tail_made")
        sum_zero, square_made, sum_made = sem("sum_zero"), sem("square_made"), sem("sum_made")
        norm_summed, rms_made, rstd_made = sem("norm_summed"), sem("rms_made"), sem("rstd_made")
        silu_made, hid_made = sem("silu_made"), sem("hid_made")
        hid_head_made, hid_tail_made = sem("hid_head_made"), sem("hid_tail_made")
        dve_chain = sem("dve_chain")
        pool_chain, act_chain = sem("pool_chain"), sem("act_chain")
        lru_consts, lam_exp = sem("lru_consts"), sem("lam_exp")
        k_windows, v_turned, v_kept = sem("k_windows"), sem("v_turned"), sem("v_kept")
        scores_made, bias_made = sem("scores_made"), sem("bias_made")
        exp_made, prob_made = sem("exp_made"), sem("prob_made")
        p_turned, p_kept, pm_kept = sem("p_turned"), sem("p_kept"), sem("pm_kept")
        pv_made, ya_kept, ya_squared = sem("pv_made"), sem("ya_kept"), sem("ya_squared")
        conv_made, ri_summed, ix_made = sem("conv_made"), sem("ri_summed"), sem("ix_made")
        a_made, om_made, root_made, u_made = sem("a_made"), sem("om_made"), sem("root_made"), sem("u_made")
        branch_sq, branch_in, branch_tanh = sem("branch_sq"), sem("branch_in"), sem("branch_tanh")
        yl_made, yl_squared = sem("yl_made"), sem("yl_squared")
        ya_head_made, ya_tail_made = sem("ya_head_made"), sem("ya_tail_made")
        yl_head_made, yl_tail_made = sem("yl_head_made"), sem("yl_tail_made")
        h_attn = sem("h_attn")
        out_made, stored = sem("out_made"), sem("stored")

        def unit_tiles(n):
            return HJ if (U_DOWN[0] <= n < U_IN or n >= U_DOWN[1]) else KD

        def col(name, i):
            return vec[:, VEC[name] + i:VEC[name] + i + 1]

        def plus(n, i, per):
            return n if i is None else i * per + n

        def block_of(t, k, i=None, per=0, cols=slice(0, L)):
            if i is None:
                return t[:, k, cols]
            return t[:, bass.ds(i * per + k, 1), cols].rearrange("p a n -> p (a n)")

        def by_piece(ap, pieces):
            return ap.rearrange("p (a n) -> p a n", a=len(pieces))

        def banks(pr, pieces):
            return pr[:, 0:len(pieces), 0:pieces[0][2]]

        def span(pieces):
            return slice(pieces[0][1], L)

        def reads_of(o):
            return o // 2 + 1

        SUM_FFN1, SUM_MIX, SUM_ATTN, SUM_LRU, SUM_FFN2, SUM_FINAL = range(1, 7)
        block = ctx.enter_context(nc.Block())

        @block.sync
        def _(sp):
            def load(n, src, i=None):
                if n >= RAW:
                    sp.wait_ge(head_made, plus(n - RAW + 1, i, SLOTS))
                    sp.wait_ge(tail_made, plus(n - RAW + 1, i, SLOTS))
                sp.dma_start(w_raw[:, n % RAW, 0:unit_tiles(n) * P], src).then_inc(w_landed[n % RAW], 16)

            def sweep(first, u, turns, dram):
                with sp.Fori(0, turns) as i:
                    for s in range(SLOTS):
                        load(first + s, dram[bass.ds(i * SLOTS + (u + s), 1), :, :].rearrange("a p n -> (a p) n"), i)

            sp.dma_start(vec[:, :], vecs).then_inc(vec_landed, 16)
            sp.dma_start(h[:, 0, :], x_t[0, :, :]).then_inc(x_landed[0], 16)
            load(0, ffn1_gu[0, :, :])
            for k in range(1, KD):
                sp.dma_start(h[:, k, :], x_t[k, :, :]).then_inc(x_landed[k], 16)
            for u in range(1, SLOTS):
                load(u, ffn1_gu[u, :, :])
            sweep(SLOTS, SLOTS, 2 * J // SLOTS - 1, ffn1_gu)
            sweep(U_DOWN[0], 0, 2 * KD // SLOTS, ffn1_down)
            for u in range(SLOTS):
                load(U_IN + u, w_in[u, :, :])
            sp.wait_ge(mixer_const, 1)
            for half in (slice(0, 64), slice(64, P)):
                for g in range(2):
                    sp.dma_start(gate_bd[half, g, :, half], gate_w[half, g, :, :]).then_inc(bd_landed, 16)
            for u in range(SLOTS, U_OUT - U_IN):
                load(U_IN + u, w_in[u, :, :])
            for u in range(U_GU[1] - U_OUT):
                load(U_OUT + u, w_out[u, :, :])
            sweep(U_GU[1], 0, 2 * J // SLOTS, ffn2_gu)
            sweep(U_DOWN[1], 0, 2 * KD // SLOTS, ffn2_down)
            for m in range(KD):
                sp.wait_ge(out_made, m + 1)
                sp.dma_start(out_t[m, :, :], h[:, m, N_META:L]).then_inc(stored, 16)
            sp.wait_ge(stored, 16 * KD)

        @block.tensor
        def _(pe):
            def product(n, pr, tiles, rhs, pieces, i=None, start=True, stop=True, before=None, group=None):
                pe.wait_ge(head_made, plus(n + 1, i, SLOTS))
                pe.wait_ge(tail_made, plus(n + 1, i, SLOTS))
                s = n % SLOTS
                group = group or tiles
                for t in range(tiles):
                    if before is not None:
                        before(t)
                    head, tail = rhs(t)
                    w_h, w_t = w_head[:, s, t * P:(t + 1) * P], w_tail[:, s, t * P:(t + 1) * P]
                    for p, (w, x) in enumerate(((w_h, head), (w_h, tail), (w_t, head))):
                        for bank, t0, width in pieces:
                            mm = pe.matmul(pr[:, bank + t // group, 0:width], w, x[:, t0:t0 + width],
                                           start=start and p == 0 and t % group == 0,
                                           stop=stop and p == 2 and t % group == group - 1)
                mm.then_inc(units_done, 1)

            def claim(o, i=None, outputs=SLOTS):
                if o >= 2:
                    pe.wait_ge(pair_read[o % 2], plus(reads_of(o) - 1, i, outputs // 2))

            def sum_channels(dst, width, ap):
                return pe.matmul(dst[:, 0:width], ones[:, :], ap, start=True, stop=True)

            def norm_sum(v, pieces):
                pe.wait_ge(sum_made, KD * (v + 1))
                for bank, t0, width in pieces:
                    mm = sum_channels(ps_c[:, bank, :], width, sum_sq[:, t0:t0 + width])
                mm.then_inc(norm_summed, 1)

            def xg(t):
                return xg_head[:, t, :], xg_tail[:, t, :]

            def xg_ready(v):
                def before(t):
                    pe.wait_ge(xg_head_made, KD * v + t + 1)
                    pe.wait_ge(xg_tail_made, KD * v + t + 1)
                return before

            def ffn(f, pieces):
                v = 2 * f

                def four(u, i=None):
                    for s in range(SLOTS):
                        first = u + s == 0 and i is None
                        claim(O_GU[f] + u + s, i)
                        product(U_GU[f] + u + s, pair[s % 2], KD, xg, pieces, i, before=xg_ready(v) if first else None)
                        if first:
                            norm_sum(v, pieces)

                four(0)
                with pe.Fori(0, 2 * J // SLOTS - 1) as i:
                    four(SLOTS, i)

                def hid(part):
                    return lambda t: (hid_head[:, part * HJ + t, :], hid_tail[:, part * HJ + t, :])

                def hid_ready(part):
                    def before(t):
                        if part * HJ + t in (0, J - 1):
                            count = J * f + (J - 1 if part == 0 else J)
                            pe.wait_ge(hid_head_made, count)
                            pe.wait_ge(hid_tail_made, count)
                    return before

                with pe.Fori(0, 2 * KD // SLOTS) as i:
                    for s in range(SLOTS):
                        m, part = s // 2, s % 2
                        if part == 0:
                            claim(O_DOWN[f] + m, i, 2)
                        product(U_DOWN[f] + s, pair[m], HJ, hid(part), pieces, i, start=part == 0, stop=part == 1,
                                before=hid_ready(part) if m == 0 else None)

            pe.wait_ge(const_made, 1)
            ffn(0, ALL)

            def project(u, o, pieces, before=None):
                claim(o)
                product(U_IN + u, pair[o % 2], KD, xg, pieces, before=before)

            project(0, O_IN, ALL, xg_ready(1))
            norm_sum(1, ALL)
            project(1, O_IN + 1, ALL)
            project(2, O_IN + 2, REAL)
            project(3, O_IN + 3, REAL)
            pe.wait_ge(pair_read[1], reads_of(O_IN + 1))
            pe.wait_ge(mixer_const, 2)
            for c in range(1, NC):
                t0 = N_META + (c - 1) * CHUNK
                pe.transpose(ps_d[:, c // 4, (c % 4) * P:(c % 4 + 1) * P], v_t[:, t0:t0 + P], ident[:, :])
            pe.transpose(ps_c[0:N_META, 0, 0:P], v_t[:, 0:N_META], ident[:, :]).then_inc(v_turned, 1)
            project(4, O_IN + 4, REAL)
            project(5, O_IN + 5, REAL)

            def scores(c):
                if c == 0:
                    for b in range(2):
                        pe.wait_ge(pair_read[b], reads_of(O_IN + 4 + b))
                    pe.wait_ge(v_kept, 1)
                    pe.wait_ge(k_windows, 1)
                else:
                    pe.wait_ge(exp_made, c)
                w, n = max(c, 1), keys(c)
                for b in range(NB):
                    for g in range(2):
                        rows = slice(64 * g, 64 * g + 64)
                        mm = pe.matmul(ps_c[rows, b // 2, (b % 2) * KEYS:(b % 2) * KEYS + n],
                                       q_t[rows, b, c * CHUNK:(c + 1) * CHUNK], k_win[rows, w, 0:n],
                                       start=True, stop=True)
                mm.then_inc(scores_made, 1)

            def turn_probs(c):
                pe.wait_ge(prob_made, c + 1)
                if c:
                    pe.wait_ge(p_kept, c)
                    pe.wait_ge(ya_kept, c)
                n = keys(c) - N_META
                for b in range(NB):
                    pe.transpose(ps_d[0:n, 0, b * P:(b + 1) * P], prob[:, b, N_META:N_META + n], ident[:, :])
                for b in range(NB):
                    mm = pe.transpose(ps_d[0:N_META, 1, b * P:(b + 1) * P], prob[:, b, 0:N_META], ident[:, :])
                mm.then_inc(p_turned, 1)

            def values(c):
                pe.wait_ge(p_kept, c + 1)
                pe.wait_ge(pm_kept, c + 1)
                n, w = keys(c) - N_META, max(c, 1)
                for g in range(2):
                    rows = slice(64 * g, 64 * g + 64)
                    dst = ps_d[rows, 1, 0:NB * CHUNK]
                    pt = p_t[0:n, :].rearrange("k (b g q) -> k b g q", b=NB, g=2)[:, :, g, :]
                    pm = p_t_meta[:, :].rearrange("k (b g q) -> k b g q", b=NB, g=2)[:, :, g, :]
                    pe.matmul(dst, v_win[0:n, w, rows], pt, start=True, stop=False)
                    mm = pe.matmul(dst, v_meta[:, rows], pm, start=False, stop=True)
                mm.then_inc(pv_made, 1)

            def lru_gates():
                pe.wait_ge(bd_landed, 64)
                for b in range(NB):
                    pe.wait_ge(conv_made, b + 1)
                    for g in range(2):
                        claim(O_GATE + 2 * b + g)
                        for bank, t0, width in ALL:
                            mm = pe.matmul(pair[g][:, bank, 0:width], gate_bd[:, g, b, :], xc[:, b, t0:t0 + width],
                                           start=True, stop=True)
                        mm.then_inc(ri_summed, 1)

            for s in range(NC + 2):
                if s < NB:
                    project(6 + s, O_IN + 6 + s, ALL)
                elif s == NB:
                    lru_gates()
                elif s <= 2 * NB:
                    project(5 + s, O_BRANCH + s - NB - 1, REAL)
                if s >= 2:
                    values(s - 2)
                if s < NC:
                    scores(s)
                if 1 <= s <= NC:
                    turn_probs(s - 1)

            for u in range(2 * NB):
                attn = u < NB
                head, tail = (ya_head, ya_tail) if attn else (yl_head, yl_tail)

                def ready(t):
                    pe.wait_ge(ya_head_made if attn else yl_head_made, t % NB + 1)
                    pe.wait_ge(ya_tail_made if attn else yl_tail_made, t % NB + 1)
                claim(O_OUT + u)
                product(U_OUT + u, pair[u % 2], KD, lambda t: (head[:, t % NB, :], tail[:, t % NB, :]),
                        [(0, 0, SEQ)], before=ready if u % NB == 0 else None, group=NB)
                if u == 0:
                    pe.wait_ge(ya_squared, NC)
                    sum_channels(ps_c[:, 0, :], SEQ, sum_sq[:, N_META:L]).then_inc(norm_summed, 1)
                if u == NB:
                    pe.wait_ge(yl_squared, 1)
                    sum_channels(ps_c[:, 1, :], SEQ, a_sq[:, 0:SEQ]).then_inc(norm_summed, 1)

            ffn(1, REAL)
            norm_sum(3, REAL)

        @block.scalar
        def _(act):
            def split_head(n, i=None):
                cols = unit_tiles(n) * P
                act.wait_ge(w_landed[n % RAW], plus(16 * (n // RAW + 1), i, 16 * SLOTS // RAW))
                if n >= SLOTS:
                    act.wait_ge(units_done, plus(n - SLOTS + 1, i, SLOTS))
                act.activation(w_head[:, n % SLOTS, 0:cols], w_raw[:, n % RAW, 0:cols], ACT.Copy).then_inc(head_made, 1)

            def root(which, src, dst, width):
                act.wait_ge(norm_summed, which)
                act.activation(dst, src, ACT.Sqrt, scale=1.0 / width, bias=eps[:, 0:1]).then_inc(rms_made, 1)

            def ffn(f, pieces):
                cols = span(pieces)

                def four(j, n, i=None):
                    for jj in (j, j + 1):
                        act.wait_ge(pair_read[0], plus(reads_of(O_GU[f] + 2 * jj), i, 2))
                        act.activation(gate_s[:, cols], gate_s[:, cols], ACT.Silu).then_inc(silu_made, 1)
                        split_head(n + 2 * (jj - j), i)
                        act.wait_ge(hid_made, plus(J * f + jj + 1, i, 2))
                        act.activation(block_of(hid_head, jj, i, 2, cols), up_s[:, cols],
                                       ACT.Copy).then_inc(hid_head_made, 1)
                        split_head(n + 2 * (jj - j) + 1, i)

                root(SUM_FFN1 if f == 0 else SUM_FFN2, banks(ps_c, pieces), by_piece(rstd[:, cols], pieces), D_MODEL)
                with act.Fori(0, 2 * J // SLOTS - 1) as i:
                    four(0, U_GU[f] + SLOTS, i)
                four(J - 2, U_DOWN[f])

                def down(m, n, i=None):
                    if n is not None:
                        split_head(n, i)
                    if f == 0:
                        act.wait_ge(pair_read[m % 2], plus(reads_of(O_DOWN[0] + m), i, 1))
                        gain = vec[:, bass.ds(i * 2 + (VEC["mix"] + m), 1)] if i is not None else col("mix", m)
                        act.activation(block_of(xg_head, m, i, 2), block_of(h, m, i, 2), ACT.Copy,
                                       scale=gain).then_inc(xg_head_made, 1)
                    if n is not None:
                        split_head(n + 1, i)

                with act.Fori(0, 2 * KD // SLOTS - 1) as i:
                    for m in range(2):
                        down(m, U_DOWN[f] + SLOTS + 2 * m, i)
                for m in range(2):
                    down(KD - 2 + m, U_IN + 2 * m if f == 0 else None)

            act.wait_ge(const_made, 1)
            act.wait_ge(vec_landed, 16)
            for k in range(KD):
                if k < 2:
                    split_head(k)
                act.wait_ge(x_landed[k], 16)
                act.activation(xg_head[:, k, :], h[:, k, :], ACT.Copy, scale=col("ffn1", k)).then_inc(xg_head_made, 1)
                if k >= 2:
                    act.wait_ge(sum_made, k - 1)
                act.activation((gate_s, up_s)[k % 2][:, :], h[:, k, :], ACT.Square).then_inc(square_made, 1)
            split_head(2)
            split_head(3)
            ffn(0, ALL)

            act.wait_ge(lru_consts, 1)
            act.activation(small[:, 1, :], small[:, 0, :], ACT.Exp, scale=-1.0).then_inc(lam_exp, 1)
            root(SUM_MIX, banks(ps_c, ALL), by_piece(rstd[:, :], ALL), D_MODEL)
            for u in range(6):
                split_head(U_IN + SLOTS + u)
                if u == 3:
                    act.wait_ge(v_turned, 1)
                    act.activation(v_win[:, 1:NC, :].rearrange("p c d -> p (c d)"),
                                   ps_d[:, :, :].rearrange("p a n -> p (a n)")[:, P:NC * P], ACT.Copy)
                    act.activation(v_meta[:, :], ps_c[0:N_META, 0, 0:P], ACT.Copy).then_inc(v_kept, 1)

            for s in range(NC + 2):
                if s == NB:
                    for b in range(NB):
                        for g, dst in ((0, r_a), (1, i_u)):
                            act.wait_ge(ri_summed, 2 * b + g + 1)
                            act.activation(by_piece(dst[:, b, :], ALL), banks(pair[g], ALL), ACT.Sigmoid,
                                           bias=col(("ba", "bx")[g], b)).then_inc(pair_read[g], 1)
                if s < NC:
                    act.wait_ge(bias_made, s + 1)
                    if s:
                        act.wait_ge(p_turned, s)
                        act.wait_ge(prob_made, s)
                    n = keys(s)
                    for b in range(NB):
                        act.activation(prob[:, b, 0:n], ps_c[:, b // 2, (b % 2) * KEYS:(b % 2) * KEYS + n], ACT.Exp,
                                       scale=ATTN_SCALE, bias=small[:, 8, b:b + 1], accum_out=small[:, 9, b:b + 1])
                    act.activation(small[:, 11, :], small[:, 10, :], ACT.Exp).then_inc(exp_made, 1)
                if 1 <= s <= NC:
                    n = keys(s - 1) - N_META
                    act.wait_ge(p_turned, s)
                    if s > 1:
                        act.wait_ge(pv_made, s - 1)
                    act.activation(p_t[0:n, :], ps_d[0:n, 0, :], ACT.Copy).then_inc(p_kept, 1)
                if s != NB and s <= 2 * NB:
                    split_head(U_IN + 10 + (s if s < NB else s - 1))
                if s in (5, 6):
                    for b in (2 * (s - 5), 2 * (s - 5) + 1):
                        act.wait_ge(lru_consts, 2)
                        act.activation(one_m_a2[:, b, :], r_a[:, b, :], ACT.Tanh, scale=small[:, 7, b:b + 1])
                        act.activation(r_a[:, b, :], r_a[:, b, :], ACT.Exp, scale=small[:, 6, b:b + 1]).then_inc(act_chain, 1)
                        act.wait_ge(act_chain, b + 1)
                        if b:
                            act.wait_ge(om_made, b)
                        act.activation(a_sq[:, :], r_a[:, b, :], ACT.Square).then_inc(a_made, 1)
                if s == 7:
                    for b in range(NB):
                        act.wait_ge(om_made, b + 1)
                        act.activation(one_m_a2[:, b, :], one_m_a2[:, b, :], ACT.Sqrt).then_inc(root_made, 1)

            act.wait_ge(ya_kept, NC)
            for b in range(NB):
                act.activation(ya_head[:, b, :], y_attn[:, b, :], ACT.Copy, scale=col("attn", b)).then_inc(ya_head_made, 1)

            def branch(b):
                act.wait_ge(pair_read[b % 2], reads_of(O_BRANCH + b))
                if b:
                    act.wait_ge(yl_made, b)
                act.activation(a_sq[:, 0:SEQ], gelu[:, b, :], ACT.Square).then_inc(branch_sq, 1)
                act.wait_ge(branch_in, b + 1)
                act.activation(a_sq[:, 0:SEQ], a_sq[:, 0:SEQ], ACT.Tanh,
                               scale=math.sqrt(2.0 / math.pi) * 0.044715).then_inc(branch_tanh, 1)

            branch(0)
            branch(1)
            root(SUM_ATTN, ps_c[:, 0, :], rstd_attn, ATTN_WIDTH)
            branch(2)
            branch(3)
            for b in range(NB):
                act.wait_ge(yl_made, b + 1)
                act.activation(yl_head[:, b, :], r_a[:, b, 0:SEQ], ACT.Copy, scale=col("lru", b)).then_inc(yl_head_made, 1)
                split_head(U_OUT + NB + b)
            root(SUM_LRU, ps_c[:, 1, :], rstd[:, N_META:L], LRU_WIDTH)
            for u in range(NB):
                split_head(U_GU[1] + u)
                act.wait_ge(h_ready, u + 1)
                for k in (2 * u, 2 * u + 1):
                    act.activation(xg_head[:, k, N_META:L], h[:, k, N_META:L], ACT.Copy,
                                   scale=col("ffn2", k)).then_inc(xg_head_made, 1)
            ffn(1, REAL)
            root(SUM_FINAL, ps_c[:, 0, :], rstd[:, N_META:L], D_MODEL)

        @block.vector
        def _(dve):
            chained = [0]

            def chain(ins):
                chained[0] += 1
                ins.then_inc(dve_chain, 1)
                dve.wait_ge(dve_chain, chained[0])

            def split_tail(n, i=None):
                cols = unit_tiles(n) * P
                dve.wait_ge(head_made, plus(n + 1, i, SLOTS))
                dve.tensor_tensor(w_tail[:, n % SLOTS, 0:cols], w_raw[:, n % RAW, 0:cols],
                                  w_head[:, n % SLOTS, 0:cols].bitcast(F32), ALU.subtract).then_inc(tail_made, 1)

            def tail_of(dst, src, gain, head):
                return dve.scalar_tensor_tensor(out=dst, in0=src, scalar=gain, in1=head.bitcast(F32),
                                                op0=ALU.mult, op1=ALU.subtract)

            def invert(which, ap):
                dve.wait_ge(rms_made, which)
                dve.reciprocal(ap, ap).then_inc(rstd_made, 1)
                dve.wait_ge(rstd_made, which)

            def scaled(o, dst, pieces, i=None):
                dve.tensor_tensor(by_piece(dst, pieces), banks(pair[o % 2], pieces),
                                  by_piece(rstd[:, span(pieces)], pieces), ALU.mult).then_inc(pair_read[o % 2], 1)

            def ffn(f, pieces):
                cols = span(pieces)

                def four(j, n, i=None):
                    for jj in (j, j + 1):
                        dve.wait_ge(units_done, plus(U_GU[f] + 2 * jj + 1, i, SLOTS))
                        if jj:
                            dve.wait_ge(hid_made, plus(J * f + jj, i, 2))
                        scaled(O_GU[f] + 2 * jj, gate_s[:, cols], pieces)
                        split_tail(n + 2 * (jj - j), i)
                        dve.wait_ge(units_done, plus(U_GU[f] + 2 * jj + 2, i, SLOTS))
                        if jj:
                            dve.wait_ge(hid_tail_made, plus(J * f + jj, i, 2))
                        scaled(O_GU[f] + 2 * jj + 1, up_s[:, cols], pieces)
                        split_tail(n + 2 * (jj - j) + 1, i)

                invert(SUM_FFN1 if f == 0 else SUM_FFN2, rstd[:, cols])
                four(0, U_GU[f] + SLOTS)
                with dve.Fori(0, 2 * J // SLOTS - 2) as i:
                    four(2, U_GU[f] + 2 * SLOTS, i)
                four(J - 2, U_DOWN[f])

                def down(m, n, i=None):
                    if n is not None:
                        split_tail(n, i)
                    o = O_DOWN[f] + m
                    dve.wait_ge(units_done, plus(U_DOWN[f] + 2 * m + 2, i, SLOTS))
                    hm = block_of(h, m, i, 2, cols)
                    dve.scalar_tensor_tensor(out=by_piece(hm, pieces), in0=banks(pair[m % 2], pieces), scalar=0.5,
                                             in1=by_piece(hm, pieces), op0=ALU.mult,
                                             op1=ALU.add).then_inc(pair_read[m % 2], 1)
                    if n is not None:
                        split_tail(n + 1, i)
                    if f == 0:
                        dve.wait_ge(pair_read[m % 2], plus(reads_of(o), i, 1))
                        dve.wait_ge(xg_head_made, plus(KD + m + 1, i, 2))
                        gain = vec[:, bass.ds(i * 2 + (VEC["mix"] + m), 1)] if i is not None else col("mix", m)
                        tail_of(block_of(xg_tail, m, i, 2), hm, gain, block_of(xg_head, m, i, 2)).then_inc(xg_tail_made, 1)

                with dve.Fori(0, 2 * KD // SLOTS - 1) as i:
                    for m in range(2):
                        down(m, U_DOWN[f] + SLOTS + 2 * m, i)
                for m in range(2):
                    down(KD - 2 + m, U_IN + 2 * m if f == 0 else None)

            dve.wait_ge(vec_landed, 16)
            for k in range(KD):
                if k < 2:
                    split_tail(k)
                dve.wait_ge(x_landed[k], 16)
                dve.wait_ge(xg_head_made, k + 1)
                tail_of(xg_tail[:, k, :], h[:, k, :], col("ffn1", k), xg_head[:, k, :]).then_inc(xg_tail_made, 1)
            split_tail(2)
            split_tail(3)
            ffn(0, ALL)

            def vcols(name):
                return vec[:, VEC[name]:VEC[name] + NB]

            def lru_exponents():
                lam, s = vcols("lam"), small
                chain(dve.tensor_scalar(s[:, 2, :], lam, -1.0, None, ALU.mult))
                dve.tensor_tensor(s[:, 0, :], lam, s[:, 2, :], ALU.max).then_inc(lru_consts, 1)
                dve.wait_ge(lam_exp, 1)
                chain(dve.tensor_scalar(s[:, 2, :], s[:, 1, :], 2.0, None, ALU.add))
                chain(dve.reciprocal(s[:, 3, :], s[:, 2, :]))
                chain(dve.tensor_tensor(s[:, 2, :], s[:, 1, :], s[:, 3, :], ALU.mult))
                chain(dve.tensor_tensor(s[:, 3, :], s[:, 2, :], s[:, 2, :], ALU.mult))
                chain(dve.tensor_scalar(s[:, 4, :], s[:, 3, :], 1.0 / 17.0, None, ALU.mult))
                for n in range(15, 1, -2):
                    chain(dve.scalar_tensor_tensor(out=s[:, 4, :], in0=s[:, 4, :], scalar=1.0 / n, in1=s[:, 3, :],
                                                   op0=ALU.add, op1=ALU.mult))
                chain(dve.scalar_tensor_tensor(out=s[:, 4, :], in0=s[:, 4, :], scalar=1.0, in1=s[:, 2, :],
                                               op0=ALU.add, op1=ALU.mult))
                chain(dve.tensor_scalar(s[:, 5, :], lam, -1.0, 0.0, ALU.mult, ALU.max))
                chain(dve.scalar_tensor_tensor(out=s[:, 5, :], in0=s[:, 4, :], scalar=2.0, in1=s[:, 5, :],
                                               op0=ALU.mult, op1=ALU.add))
                dve.tensor_scalar(s[:, 6, :], s[:, 5, :], -LRU_C, None, ALU.mult)
                dve.tensor_scalar(s[:, 7, :], s[:, 5, :], LRU_C, None, ALU.mult).then_inc(lru_consts, 1)
                chain(dve.tensor_scalar(s[:, 12, :], vcols("sink"), -1.0, None, ALU.mult))

            dve.wait_ge(units_done, U_IN)
            lru_exponents()
            invert(SUM_MIX, rstd[:, :])
            for u in range(6):
                dve.wait_ge(units_done, U_IN + u + 1)
                if u < 2:
                    scaled(O_IN + u, (k_t, v_t)[u][:, :], ALL)
                else:
                    scaled(O_IN + u, q_t[:, u - 2, :], REAL)
                split_tail(U_IN + SLOTS + u)
                if u == 0:
                    dve.wait_ge(pair_read[0], reads_of(O_IN))
                    w = NC - 1
                    chunks = k_t[:, N_META:L].rearrange("p (w n) -> p w n", w=NC)
                    dve.tensor_copy(k_win[:, 1:NC, N_META:N_META + CHUNK], chunks[:, 0:w, :])
                    dve.tensor_copy(k_win[:, 1:NC, N_META + CHUNK:KEYS], chunks[:, 1:NC, :])
                    dve.tensor_copy(k_win[:, 1:NC, 0:N_META],
                                    k_t[:, 0:N_META].unsqueeze(1).broadcast_to([P, w, N_META])).then_inc(k_windows, 1)

            for s in range(NC + 2):
                if s < NB:
                    b = s
                    dve.wait_ge(units_done, U_IN + 7 + s)
                    dve.wait_ge(mixer_const, 3)
                    scaled(O_IN + 6 + s, x_pad[:, CONV_WIDTH - 1:], ALL)
                    dve.wait_ge(pair_read[s % 2], reads_of(O_IN + 6 + s))
                    last = CONV_WIDTH - 1
                    ins = dve.tensor_scalar(xc[:, b, :], x_pad[:, last:last + L], col("conv_w", last * NB + b),
                                            col("conv_b", b), ALU.mult, ALU.add)
                    for tap in range(last - 1, -1, -1):
                        chain(ins)
                        ins = dve.scalar_tensor_tensor(out=xc[:, b, :], in0=x_pad[:, tap:tap + L],
                                                       scalar=col("conv_w", tap * NB + b), in1=xc[:, b, :],
                                                       op0=ALU.mult, op1=ALU.add)
                    ins.then_inc(conv_made, 1)
                elif NB < s <= 2 * NB:
                    b = s - NB - 1
                    dve.wait_ge(units_done, U_IN + 11 + b)
                    scaled(O_BRANCH + b, gelu[:, b, :], REAL)
                if s >= 2:
                    c = s - 2
                    dve.wait_ge(pv_made, c + 1)
                    dve.tensor_copy(y_attn[:, :, c * CHUNK:(c + 1) * CHUNK],
                                    ps_d[:, 1, 0:NB * CHUNK].rearrange("p (b q) -> p b q", b=NB)).then_inc(ya_kept, 1)
                if s < NC:
                    n = keys(s)
                    dve.wait_ge(scores_made, s + 1)
                    chain(dve.tensor_reduce(small[:, 13, :].rearrange("p (a b) -> p a b", a=2),
                                            ps_c[:, :, 0:2 * KEYS].rearrange("p a (b n) -> p a b n", b=2)[:, :, :, 0:n],
                                            AX_X, ALU.max))
                    chain(dve.scalar_tensor_tensor(out=small[:, 8, :], in0=small[:, 13, :], scalar=-ATTN_SCALE,
                                                   in1=small[:, 12, :], op0=ALU.mult, op1=ALU.min))
                    dve.tensor_tensor(small[:, 10, :], vcols("sink"), small[:, 8, :], ALU.add).then_inc(bias_made, 1)
                if 1 <= s <= NC:
                    dve.wait_ge(p_turned, s)
                    if s > 1:
                        dve.wait_ge(pv_made, s - 1)
                    dve.tensor_copy(p_t_meta[:, :], ps_d[0:N_META, 1, :]).then_inc(pm_kept, 1)
                if s != NB and s <= 2 * NB:
                    split_tail(U_IN + 10 + (s if s < NB else s - 1))
                if s < NC:
                    dve.wait_ge(exp_made, s + 1)
                    chain(dve.tensor_tensor(small[:, 14, :], small[:, 9, :], small[:, 11, :], ALU.add))
                    chain(dve.reciprocal(small[:, 15, :], small[:, 14, :]))
                    dve.tensor_tensor(prob[:, :, 0:n], prob[:, :, 0:n],
                                      small[:, 15, :].unsqueeze(2).broadcast_to([P, NB, n]),
                                      ALU.mult).then_inc(prob_made, 1)
                if s in (5, 6):
                    for b in (2 * (s - 5), 2 * (s - 5) + 1):
                        dve.wait_ge(a_made, b + 1)
                        dve.scalar_tensor_tensor(out=one_m_a2[:, b, :], in0=a_sq[:, :], scalar=1.0,
                                                 in1=one_m_a2[:, b, :], op0=ALU.add, op1=ALU.mult).then_inc(om_made, 1)
                if s == 8:
                    for b in range(NB):
                        dve.wait_ge(u_made, b + 1)
                        chain(dve.tensor_tensor_scan(xc[:, b, :], r_a[:, b, :], i_u[:, b, :], 0.0, ALU.mult, ALU.add))

            for b in range(NB):
                dve.wait_ge(ya_head_made, b + 1)
                tail_of(ya_tail[:, b, :], y_attn[:, b, :], col("attn", b), ya_head[:, b, :]).then_inc(ya_tail_made, 1)

            def branch(b):
                dve.wait_ge(branch_sq, b + 1)
                dve.scalar_tensor_tensor(out=a_sq[:, 0:SEQ], in0=a_sq[:, 0:SEQ], scalar=1.0 / 0.044715,
                                         in1=gelu[:, b, :], op0=ALU.add, op1=ALU.mult).then_inc(branch_in, 1)
                dve.wait_ge(branch_tanh, b + 1)
                chain(dve.scalar_tensor_tensor(out=gelu[:, b, :], in0=a_sq[:, 0:SEQ], scalar=1.0, in1=gelu[:, b, :],
                                               op0=ALU.add, op1=ALU.mult))
                dve.scalar_tensor_tensor(out=r_a[:, b, 0:SEQ], in0=gelu[:, b, :], scalar=0.5, in1=xc[:, b, N_META:L],
                                         op0=ALU.mult, op1=ALU.mult).then_inc(yl_made, 1)

            def out_step(u, factor):
                dve.wait_ge(units_done, U_OUT + u + 1)
                if u:
                    dve.wait_ge(h_attn if u <= NB else h_ready, u if u <= NB else u - NB)
                dve.tensor_tensor(y_scaled[:, :, :], pair[u % 2][:, :, :],
                                  factor.unsqueeze(1).broadcast_to([P, 2, SEQ]), ALU.mult).then_inc(pair_read[u % 2], 1)
                dve.wait_ge(pair_read[u % 2], reads_of(O_OUT + u))
                k = 2 * (u % NB)
                ins = dve.tensor_tensor(h[:, k:k + 2, N_META:L], h[:, k:k + 2, N_META:L], y_scaled[:, :, :], ALU.add)
                ins.then_inc(h_ready if u >= NB else h_attn, 1)

            branch(0)
            branch(1)
            invert(SUM_ATTN, rstd_attn)
            out_step(0, rstd_attn)
            branch(2)
            branch(3)
            for b in range(NB):
                dve.wait_ge(yl_head_made, b + 1)
                tail_of(yl_tail[:, b, :], r_a[:, b, 0:SEQ], col("lru", b), yl_head[:, b, :]).then_inc(yl_tail_made, 1)
                split_tail(U_OUT + NB + b)
                if b:
                    out_step(b, rstd_attn)
            invert(SUM_LRU, rstd[:, N_META:L])
            for u in range(NB):
                dve.wait_ge(h_attn, NB)
                out_step(NB + u, rstd[:, N_META:L])
                split_tail(U_GU[1] + u)
                dve.wait_ge(h_ready, u + 1)
                for k in (2 * u, 2 * u + 1):
                    dve.wait_ge(xg_head_made, 2 * KD + k + 1)
                    tail_of(xg_tail[:, k, N_META:L], h[:, k, N_META:L], col("ffn2", k),
                            xg_head[:, k, N_META:L]).then_inc(xg_tail_made, 1)
            ffn(1, REAL)

            invert(SUM_FINAL, rstd[:, N_META:L])
            for m in range(KD):
                dve.scalar_tensor_tensor(out=h[:, m, N_META:L], in0=h[:, m, N_META:L], scalar=col("final", m),
                                         in1=rstd[:, N_META:L], op0=ALU.mult, op1=ALU.mult).then_inc(out_made, 1)

        @block.gpsimd
        def _(pool):
            chained = [0]

            def chain(ins):
                chained[0] += 1
                ins.then_inc(pool_chain, 1)
                pool.wait_ge(pool_chain, chained[0])

            def identity():
                chain(pool.memset(ident[:, :], 0.0))
                pool.affine_select(out=ident[:, :], in_=ident[:, :], compare_op=ALU.not_equal, fill=1.0, base=0,
                                   pattern=[[-1, P]], channel_multiplier=1).then_inc(mixer_const, 1)

            def clear_sum(which):
                if which > 1:
                    pool.wait_ge(norm_summed, which - 1)
                pool.memset(sum_sq[:, :], 0.0).then_inc(sum_zero, 1)
                pool.wait_ge(sum_zero, {SUM_FFN1: 1, SUM_MIX: 2, SUM_FFN2: 3, SUM_FINAL: 4}[which])

            def add_square(v, k, cols, i=None):
                hk = block_of(h, k, i, 2, cols)
                pool.tensor_tensor(square[:, cols], hk, hk, ALU.mult).then_inc(square_made, 1)
                pool.wait_ge(square_made, plus(KD * v + k + 1, i, 2))
                pool.tensor_tensor(sum_sq[:, cols], sum_sq[:, cols], square[:, cols], ALU.add).then_inc(sum_made, 1)
                pool.wait_ge(sum_made, plus(KD * v + k + 1, i, 2))

            def ffn(f, pieces):
                cols = span(pieces)
                with pool.Fori(0, J) as i:
                    o = O_GU[f]
                    pool.wait_ge(silu_made, plus(J * f + 1, i, 1))
                    pool.wait_ge(pair_read[1], plus(reads_of(o + 1), i, 1))
                    pool.tensor_tensor(up_s[:, cols], gate_s[:, cols], up_s[:, cols], ALU.mult).then_inc(hid_made, 1)
                    pool.wait_ge(hid_head_made, plus(J * f + 1, i, 1))
                    pool.tensor_tensor(block_of(hid_tail, 0, i, 1, cols), up_s[:, cols],
                                       block_of(hid_head, 0, i, 1, cols).bitcast(F32),
                                       ALU.subtract).then_inc(hid_tail_made, 1)
                v = 2 * f + 1
                clear_sum(SUM_MIX if f == 0 else SUM_FINAL)
                with pool.Fori(0, KD // 2) as i:
                    for m in range(2):
                        pool.wait_ge(pair_read[m], plus(reads_of(O_DOWN[f] + m), i, 1))
                        add_square(v, m, cols, i)

            pool.memset(ones[:, :], 1.0)
            pool.memset(eps[:, :], EPS).then_inc(const_made, 1)
            clear_sum(SUM_FFN1)
            for k in range(KD):
                pool.wait_ge(square_made, k + 1)
                pool.tensor_tensor(sum_sq[:, :], sum_sq[:, :], (gate_s, up_s)[k % 2][:, :], ALU.add).then_inc(sum_made, 1)
                pool.wait_ge(sum_made, k + 1)
            ffn(0, ALL)

            pool.wait_ge(units_done, U_IN)
            pool.memset(gate_bd[:, :, :, :], 0.0).then_inc(mixer_const, 1)
            identity()
            pool.memset(x_pad[:, 0:CONV_WIDTH - 1], 0.0).then_inc(mixer_const, 1)

            pool.wait_ge(norm_summed, SUM_MIX)
            for s in range(2, NC + 3):
                if s < NC + 2:
                    c = s - 2
                    t0 = c * CHUNK
                    pool.wait_ge(ya_kept, c + 1)
                    sq = square[:, 0:NB * CHUNK].rearrange("p (b q) -> p b q", b=NB)
                    two = square[:, NB * CHUNK:NB * CHUNK + 2 * CHUNK].rearrange("p (b q) -> p b q", b=2)
                    yc = y_attn[:, :, t0:t0 + CHUNK]
                    chain(pool.tensor_tensor(sq, yc, yc, ALU.mult))
                    chain(pool.tensor_tensor(two, sq[:, 0:2, :], sq[:, 2:4, :], ALU.add))
                    pool.tensor_tensor(sum_sq[:, N_META + t0:N_META + t0 + CHUNK], two[:, 0, :], two[:, 1, :],
                                       ALU.add).then_inc(ya_squared, 1)
                if s == NB:
                    for b in range(NB):
                        pool.wait_ge(pair_read[1], reads_of(O_GATE + 2 * b + 1))
                        pool.wait_ge(conv_made, b + 1)
                        pool.tensor_tensor(i_u[:, b, :], i_u[:, b, :], xc[:, b, :], ALU.mult).then_inc(ix_made, 1)
                if s == 7:
                    for b in range(NB):
                        pool.wait_ge(ix_made, b + 1)
                        pool.wait_ge(root_made, b + 1)
                        pool.tensor_tensor(i_u[:, b, :], i_u[:, b, :], one_m_a2[:, b, :], ALU.mult).then_inc(u_made, 1)
            pool.wait_ge(yl_made, NB)
            lru_sum = a_sq[:, 0:SEQ]
            for b in range(NB):
                yb = r_a[:, b, 0:SEQ]
                if b == 0:
                    ins = pool.tensor_tensor(lru_sum, yb, yb, ALU.mult)
                else:
                    chain(pool.tensor_tensor(square[:, 0:SEQ], yb, yb, ALU.mult))
                    ins = pool.tensor_tensor(lru_sum, lru_sum, square[:, 0:SEQ], ALU.add)
                if b < NB - 1:
                    chain(ins)
                else:
                    ins.then_inc(yl_squared, 1)

            clear_sum(SUM_FFN2)
            for k in range(KD):
                pool.wait_ge(h_ready, k // 2 + 1)
                add_square(2, k, slice(N_META, L))
            ffn(1, REAL)


def kernel(x, meta_tokens, ffn1_norm, ffn1_w_gate, ffn1_w_up, ffn1_w_down, mix_norm, w_in, attn_sinks, conv_w, conv_b,
           lru_wa, lru_ba, lru_wx, lru_bx, lru_lambda, attn_out_norm, lru_out_norm, w_out, ffn2_norm, ffn2_w_gate,
           ffn2_w_up, ffn2_w_down, final_norm):
    import numpy as np

    import concourse.bacc as bacc
    from concourse.bass_utils import run_bass_kernel_spmd

    def tiles(w, rows, cols):
        return np.asarray(w).reshape(rows, P, cols, P).transpose(0, 2, 1, 3)

    def units(t):
        return np.ascontiguousarray(t.transpose(0, 2, 1, 3).reshape(t.shape[0], P, t.shape[1] * P))

    def gate_up(gate, up):
        both = np.stack([tiles(gate[0], KD, J), tiles(up[0], KD, J)])
        return units(both.transpose(2, 0, 1, 3, 4).reshape(2 * J, KD, P, P))

    def down(w):
        t = tiles(w[0], J, KD).reshape(2, HJ, KD, P, P)
        return units(t.transpose(2, 0, 1, 3, 4).reshape(2 * KD, HJ, P, P))

    def columns(a):
        return np.asarray(a).reshape(-1, P).T

    heads = np.arange(ATTN_WIDTH).reshape(2, NB, HEAD_DIM).transpose(1, 0, 2).reshape(-1)
    w = np.asarray(w_in[0])
    q, k, v, x_lru, branch = np.split(w, np.cumsum([ATTN_WIDTH, P, P, LRU_WIDTH]), axis=1)
    w_in_units = units(tiles(np.concatenate([k, v, q[:, heads], x_lru, branch], axis=1), KD, U_OUT - U_IN)
                       .transpose(1, 0, 2, 3))
    w = np.asarray(w_out[0])
    w = np.concatenate([w[0:ATTN_WIDTH][heads], w[ATTN_WIDTH:]])
    t = tiles(w, 2 * NB, KD).reshape(2, NB, KD // 2, 2, P, P)
    w_out_units = units(t.transpose(0, 2, 3, 1, 4, 5).reshape(2 * NB, KD, P, P))

    def gates(a):
        return np.asarray(a[0]).reshape(NB, P, 64).transpose(1, 0, 2)

    sinks = np.repeat(np.asarray(attn_sinks[0]).reshape(2, NB), 64, axis=0)
    vecs = np.concatenate([columns(a) for a in (
        ffn1_norm[0], mix_norm[0], ffn2_norm[0], final_norm, attn_out_norm[0][heads], lru_out_norm[0], conv_w[0],
        conv_b[0], lru_ba[0], lru_bx[0], lru_lambda[0])] + [sinks], axis=1)
    tokens = np.concatenate([np.asarray(meta_tokens), np.asarray(x[0])])
    arrays = {
        "x_t": tokens.T.reshape(KD, P, L),
        "ffn1_gu": gate_up(ffn1_w_gate, ffn1_w_up), "ffn1_down": down(ffn1_w_down),
        "w_in": w_in_units, "w_out": w_out_units,
        "ffn2_gu": gate_up(ffn2_w_gate, ffn2_w_up), "ffn2_down": down(ffn2_w_down),
        "gate_w": np.stack([gates(lru_wa), gates(lru_wx)], axis=1),
        "vecs": vecs,
    }
    arrays = {name: np.ascontiguousarray(a) for name, a in arrays.items()}
    nc = bacc.Bacc("TRN2", target_bir_lowering=False, num_devices=1)
    args = {name: nc.dram_tensor(name, a.shape, mybir.dt.from_np(a.dtype), kind="ExternalInput").ap()
            for name, a in arrays.items()}
    args["out_t"] = nc.dram_tensor("out_t", (KD, P, SEQ), F32, kind="ExternalOutput").ap()
    build_layer(nc, **args)
    r = run_bass_kernel_spmd(nc, [arrays], core_ids=[0])
    out = r.results[0]["out_t"]
    return np.ascontiguousarray(out.reshape(D_MODEL, SEQ).T)[None]
```

```python
import math
from contextlib import ExitStack

import concourse.bass as bass
from concourse import mybir

F32 = mybir.dt.float32
F32R = mybir.dt.float32r
ALU = mybir.AluOpType
ACT = mybir.ActivationFunctionType
AX_X = mybir.AxisListType.X

P = 128
D_MODEL, SEQ, N_META, D_FF = 1024, 512, 16, 2816
CHUNK, HEAD_DIM, LRU_WIDTH, CONV_WIDTH = 64, 64, 512, 4
EPS, LRU_C = 1e-6, 8.0
ATTN_SCALE = HEAD_DIM ** -0.5
L = N_META + SEQ
KD = D_MODEL // P
J = D_FF // P
HJ = J // 2
NB = LRU_WIDTH // P
NC = SEQ // CHUNK
KEYS = N_META + 2 * CHUNK
ATTN_WIDTH = NB * P
SLOTS, RAW = 4, 2

U_GU = (0, 82)
U_DOWN = (44, 126)
U_IN, U_OUT = 60, 74

O_QUERY, O_X, O_GATE, O_BRANCH, O_OUT, OUTPUTS = 2, 6, 10, 18, 22, 30
TURNS = 2 * J // SLOTS
READS_MIX = TURNS + KD // 2
READS_FFN2 = READS_MIX + OUTPUTS // 2

ALL = [(0, 0, L // 2), (1, L // 2, L // 2)]
REAL = [(0, N_META, SEQ)]

VEC = {}
_at = 0
for _name, _n in (("ffn1", KD), ("mix", KD), ("ffn2", KD), ("final", KD), ("attn", NB), ("lru", NB),
                  ("conv_w", CONV_WIDTH * NB), ("conv_b", NB), ("ba", NB), ("bx", NB), ("lam", NB), ("sink", NB)):
    VEC[_name] = _at
    _at += _n
NVEC = _at


def keys(c):
    return KEYS if c else KEYS - CHUNK


def build_layer(nc, x_t, ffn1_gu, ffn1_down, w_in, w_out, ffn2_gu, ffn2_down, gate_w, vecs, out_t):
    with ExitStack() as ctx:
        def sb(name, shape, dt=F32, where=ctx):
            return where.enter_context(nc.sbuf_tensor(name, shape, dt))

        def sem(name):
            return ctx.enter_context(nc.semaphore(name))

        h = sb("h", [P, KD, L])
        xg_head = sb("xg_head", [P, KD, L], F32R)
        xg_tail = sb("xg_tail", [P, KD, L], F32R)
        w_raw = sb("w_raw", [P, RAW, HJ * P])
        w_head = sb("w_head", [P, SLOTS, HJ * P], F32R)
        w_tail = sb("w_tail", [P, SLOTS, HJ * P], F32R)
        rstd = sb("rstd", [P, L])
        square = sb("square", [P, L])
        sum_sq = sb("sum_sq", [P, L])
        ones = sb("ones", [P, P])
        vec = sb("vec", [P, NVEC])
        eps = sb("eps", [P, 1])

        with ExitStack() as ffn:
            hid_head = sb("hid_head", [P, J, L], F32R, ffn)
            hid_tail = sb("hid_tail", [P, J, L], F32R, ffn)
            gate_s = sb("gate_s", [P, L], F32, ffn)
            up_s = sb("up_s", [P, L], F32, ffn)
        with ExitStack() as early:
            q_t = sb("q_t", [P, NB, SEQ], F32, early)
            k_win = sb("k_win", [P, NC, KEYS], F32, early)
        ya_head = sb("ya_head", [P, NB, SEQ], F32R)
        ya_tail = sb("ya_tail", [P, NB, SEQ], F32R)
        with ExitStack() as early:
            k_t = sb("k_t", [P, L], F32, early)
            v_t = sb("v_t", [P, L], F32, early)
        one_m_a2 = sb("one_m_a2", [P, NB, L])
        with ExitStack() as early:
            p_t = sb("p_t", [P, NB * P], F32, early)
            p_t_meta = sb("p_t_meta", [N_META, NB * P], F32, early)
        y_scaled = sb("y_scaled", [P, 2, SEQ])
        with ExitStack() as early:
            gelu = sb("gelu", [P, NB, SEQ], F32, early)
        yl_tail = sb("yl_tail", [P, NB, SEQ], F32R)
        yl_head = sb("yl_head", [P, NB, SEQ], F32R)
        v_win = sb("v_win", [P, NC, P])
        v_meta = sb("v_meta", [N_META, P])
        prob = sb("prob", [P, NB, KEYS])
        y_attn = sb("y_attn", [P, NB, SEQ])
        x_pad = sb("x_pad", [P, CONV_WIDTH - 1 + L])
        xc = sb("xc", [P, NB, L])
        r_a = sb("r_a", [P, NB, L])
        i_u = sb("i_u", [P, NB, L])
        a_sq = sb("a_sq", [P, L])
        gate_bd = sb("gate_bd", [P, 2, NB, P])
        ident = sb("ident", [P, P])
        small = sb("small", [P, 16, NB])
        rstd_attn = one_m_a2[:, 0, 0:SEQ]

        ps = [ctx.enter_context(nc.psum_tensor(f"ps{i}", [P, 2, 512], F32)) for i in range(4)]
        ps_c, ps_d = ps[2], ps[3]

        x_landed = [sem(f"x_landed{k}") for k in range(KD)]
        vec_landed, bd_landed = sem("vec_landed"), sem("bd_landed")
        w_landed = [sem(f"w_landed{r}") for r in range(RAW)]
        head_made, tail_made = sem("head_made"), sem("tail_made")
        units_done = sem("units_done")
        pair_read = [sem(f"pair_read{q}") for q in range(4)]
        const_made, mixer_const = sem("const_made"), sem("mixer_const")
        h_ready, xg_head_made, xg_tail_made = sem("h_ready"), sem("xg_head_made"), sem("xg_tail_made")
        sum_zero, square_made, sum_made = sem("sum_zero"), sem("square_made"), sem("sum_made")
        norm_summed, rms_made, rstd_made = sem("norm_summed"), sem("rms_made"), sem("rstd_made")
        silu_made, hid_made = sem("silu_made"), sem("hid_made")
        hid_head_made, hid_tail_made = sem("hid_head_made"), sem("hid_tail_made")
        dve_chain = sem("dve_chain")
        pool_chain, act_chain = sem("pool_chain"), sem("act_chain")
        lru_consts, lam_exp = sem("lru_consts"), sem("lam_exp")
        k_windows, v_turned, v_kept = sem("k_windows"), sem("v_turned"), sem("v_kept")
        scores_made, bias_made = sem("scores_made"), sem("bias_made")
        exp_made, prob_made = sem("exp_made"), sem("prob_made")
        p_turned, p_kept, pm_kept = sem("p_turned"), sem("p_kept"), sem("pm_kept")
        pv_made, ya_kept, ya_squared = sem("pv_made"), sem("ya_kept"), sem("ya_squared")
        conv_made, ri_summed, ix_made = sem("conv_made"), sem("ri_summed"), sem("ix_made")
        a_made, om_made, root_made, u_made = sem("a_made"), sem("om_made"), sem("root_made"), sem("u_made")
        gelu_made = sem("gelu_made")
        yl_made, yl_squared = sem("yl_made"), sem("yl_squared")
        ya_head_made, ya_tail_made = sem("ya_head_made"), sem("ya_tail_made")
        yl_head_made, yl_tail_made = sem("yl_head_made"), sem("yl_tail_made")
        h_attn = sem("h_attn")
        out_made, stored = sem("out_made"), sem("stored")

        def unit_tiles(n):
            return HJ if (U_DOWN[0] <= n < U_IN or n >= U_DOWN[1]) else KD

        def col(name, i):
            return vec[:, VEC[name] + i:VEC[name] + i + 1]

        def plus(n, i, per):
            return n if i is None else i * per + n

        def block_of(t, k, i=None, per=0, cols=slice(0, L)):
            if i is None:
                return t[:, k, cols]
            return t[:, bass.ds(i * per + k, 1), cols].rearrange("p a n -> p (a n)")

        def by_piece(ap, pieces):
            return ap.rearrange("p (a n) -> p a n", a=len(pieces))

        def banks(pr, pieces):
            return pr[:, 0:len(pieces), 0:pieces[0][2]]

        def span(pieces):
            return slice(pieces[0][1], L)

        def gu_place(f, u):
            q = (0, 1, 3, 2)[u % SLOTS]
            return q, (0, READS_FFN2 if q < 2 else TURNS)[f] + u // SLOTS

        def down_place(f, m):
            return m % 2, (0, READS_FFN2)[f] + TURNS + m // 2

        def mix_place(o):
            return o % 2, READS_MIX + o // 2

        def wait_read(eng, place, i=None, more=1):
            q, before = place
            if before + more > 0:
                eng.wait_ge(pair_read[q], plus(before + more, i, 1))

        SUM_FFN1, SUM_MIX, SUM_ATTN, SUM_LRU, SUM_FFN2, SUM_FINAL = range(1, 7)
        block = ctx.enter_context(nc.Block())

        @block.sync
        def _(sp):
            def load(n, src, i=None):
                if n >= RAW:
                    sp.wait_ge(head_made, plus(n - RAW + 1, i, SLOTS))
                    sp.wait_ge(tail_made, plus(n - RAW + 1, i, SLOTS))
                sp.dma_start(w_raw[:, n % RAW, 0:unit_tiles(n) * P], src).then_inc(w_landed[n % RAW], 16)

            def sweep(first, u, turns, dram):
                with sp.Fori(0, turns) as i:
                    for s in range(SLOTS):
                        load(first + s, dram[bass.ds(i * SLOTS + (u + s), 1), :, :].rearrange("a p n -> (a p) n"), i)

            sp.dma_start(vec[:, :], vecs).then_inc(vec_landed, 16)
            sp.dma_start(h[:, 0, :], x_t[0, :, :]).then_inc(x_landed[0], 16)
            load(0, ffn1_gu[0, :, :])
            for k in range(1, KD):
                sp.dma_start(h[:, k, :], x_t[k, :, :]).then_inc(x_landed[k], 16)
            for u in range(1, SLOTS):
                load(u, ffn1_gu[u, :, :])
            sweep(SLOTS, SLOTS, 2 * J // SLOTS - 1, ffn1_gu)
            sweep(U_DOWN[0], 0, 2 * KD // SLOTS, ffn1_down)
            for u in range(SLOTS):
                load(U_IN + u, w_in[u, :, :])
            sp.wait_ge(mixer_const, 1)
            for half in (slice(0, 64), slice(64, P)):
                for g in range(2):
                    sp.dma_start(gate_bd[half, g, :, half], gate_w[half, g, :, :]).then_inc(bd_landed, 16)
            for u in range(SLOTS, U_OUT - U_IN):
                load(U_IN + u, w_in[u, :, :])
            for u in range(U_GU[1] - U_OUT):
                load(U_OUT + u, w_out[u, :, :])
            sweep(U_GU[1], 0, 2 * J // SLOTS, ffn2_gu)
            sweep(U_DOWN[1], 0, 2 * KD // SLOTS, ffn2_down)
            for m in range(KD):
                sp.wait_ge(out_made, m + 1)
                sp.dma_start(out_t[m, :, :], h[:, m, N_META:L]).then_inc(stored, 16)
            sp.wait_ge(stored, 16 * KD)

        @block.tensor
        def _(pe):
            def product(n, pr, tiles, rhs, pieces, i=None, start=True, stop=True, before=None, group=None):
                pe.wait_ge(head_made, plus(n + 1, i, SLOTS))
                pe.wait_ge(tail_made, plus(n + 1, i, SLOTS))
                s = n % SLOTS
                group = group or tiles
                for t in range(tiles):
                    if before is not None:
                        before(t)
                    head, tail = rhs(t)
                    w_h, w_t = w_head[:, s, t * P:(t + 1) * P], w_tail[:, s, t * P:(t + 1) * P]
                    for p, (w, x) in enumerate(((w_h, head), (w_h, tail), (w_t, head))):
                        for bank, t0, width in pieces:
                            mm = pe.matmul(pr[:, bank + t // group, 0:width], w, x[:, t0:t0 + width],
                                           start=start and p == 0 and t % group == 0,
                                           stop=stop and p == 2 and t % group == group - 1)
                mm.then_inc(units_done, 1)

            def sum_channels(dst, width, ap):
                return pe.matmul(dst[:, 0:width], ones[:, :], ap, start=True, stop=True)

            def norm_sum(v, pieces):
                pe.wait_ge(sum_made, KD * (v + 1))
                for bank, t0, width in pieces:
                    mm = sum_channels(ps_c[:, bank, :], width, sum_sq[:, t0:t0 + width])
                mm.then_inc(norm_summed, 1)

            def xg(t):
                return xg_head[:, t, :], xg_tail[:, t, :]

            def xg_ready(v):
                def before(t):
                    pe.wait_ge(xg_head_made, KD * v + t + 1)
                    pe.wait_ge(xg_tail_made, KD * v + t + 1)
                return before

            def ffn(f, pieces):
                v = 2 * f

                def four(u, i=None):
                    first = i is None
                    for s in range(SLOTS):
                        place = gu_place(f, u + s)
                        if first and s == SLOTS - 1:
                            pe.wait_ge(rms_made, SUM_FFN1 if f == 0 else SUM_FFN2)
                        wait_read(pe, place, i, more=0)
                        product(U_GU[f] + u + s, ps[place[0]], KD, xg, pieces, i,
                                before=xg_ready(v) if first and s == 0 else None)
                        if first and s == 1:
                            norm_sum(v, pieces)

                four(0)
                with pe.Fori(0, TURNS - 1) as i:
                    four(SLOTS, i)

                def hid(part):
                    return lambda t: (hid_head[:, part * HJ + t, :], hid_tail[:, part * HJ + t, :])

                def hid_ready(part):
                    def before(t):
                        if part * HJ + t in (0, J - 1):
                            count = J * f + (J - 1 if part == 0 else J)
                            pe.wait_ge(hid_head_made, count)
                            pe.wait_ge(hid_tail_made, count)
                    return before

                with pe.Fori(0, 2 * KD // SLOTS) as i:
                    for s in range(SLOTS):
                        m, part = s // 2, s % 2
                        if part == 0:
                            wait_read(pe, down_place(f, m), i, more=0)
                        product(U_DOWN[f] + s, ps[m], HJ, hid(part), pieces, i, start=part == 0, stop=part == 1,
                                before=hid_ready(part) if m == 0 else None)

            pe.wait_ge(const_made, 1)
            ffn(0, ALL)

            def project(u, pieces, before=None, o=None):
                place = mix_place(u if o is None else o)
                wait_read(pe, place, more=0)
                product(U_IN + u, ps[place[0]], KD, xg, pieces, before=before)

            project(0, ALL, xg_ready(1))
            norm_sum(1, ALL)
            project(1, ALL)
            project(2, REAL)
            project(3, REAL)
            wait_read(pe, mix_place(1))
            pe.wait_ge(mixer_const, 2)
            for c in range(1, NC):
                t0 = N_META + (c - 1) * CHUNK
                pe.transpose(ps_d[:, c // 4, (c % 4) * P:(c % 4 + 1) * P], v_t[:, t0:t0 + P], ident[:, :])
            pe.transpose(ps_c[0:N_META, 0, 0:P], v_t[:, 0:N_META], ident[:, :]).then_inc(v_turned, 1)
            project(4, REAL)

            def scores(c):
                if c == 0:
                    for b in range(2):
                        wait_read(pe, mix_place(O_QUERY + 2 + b))
                    pe.wait_ge(v_kept, 1)
                    pe.wait_ge(k_windows, 1)
                else:
                    pe.wait_ge(exp_made, c)
                w, n = max(c, 1), keys(c)
                for b in range(NB):
                    for g in range(2):
                        rows = slice(64 * g, 64 * g + 64)
                        mm = pe.matmul(ps_c[rows, b // 2, (b % 2) * KEYS:(b % 2) * KEYS + n],
                                       q_t[rows, b, c * CHUNK:(c + 1) * CHUNK], k_win[rows, w, 0:n],
                                       start=True, stop=True)
                mm.then_inc(scores_made, 1)

            def turn_probs(c):
                pe.wait_ge(prob_made, c + 1)
                if c:
                    pe.wait_ge(p_kept, c)
                    pe.wait_ge(ya_kept, c)
                n = keys(c) - N_META
                for b in range(NB):
                    pe.transpose(ps_d[0:n, 0, b * P:(b + 1) * P], prob[:, b, N_META:N_META + n], ident[:, :])
                for b in range(NB):
                    mm = pe.transpose(ps_d[0:N_META, 1, b * P:(b + 1) * P], prob[:, b, 0:N_META], ident[:, :])
                mm.then_inc(p_turned, 1)

            def values(c):
                pe.wait_ge(p_kept, c + 1)
                pe.wait_ge(pm_kept, c + 1)
                n, w = keys(c) - N_META, max(c, 1)
                for g in range(2):
                    rows = slice(64 * g, 64 * g + 64)
                    dst = ps_d[rows, 1, 0:NB * CHUNK]
                    pt = p_t[0:n, :].rearrange("k (b g q) -> k b g q", b=NB, g=2)[:, :, g, :]
                    pm = p_t_meta[:, :].rearrange("k (b g q) -> k b g q", b=NB, g=2)[:, :, g, :]
                    pe.matmul(dst, v_win[0:n, w, rows], pt, start=True, stop=False)
                    mm = pe.matmul(dst, v_meta[:, rows], pm, start=False, stop=True)
                mm.then_inc(pv_made, 1)

            def lru_gates(b):
                pe.wait_ge(bd_landed, 64)
                pe.wait_ge(conv_made, b + 1)
                for g in range(2):
                    wait_read(pe, mix_place(O_GATE + 2 * b + g), more=0)
                    for bank, t0, width in ALL:
                        mm = pe.matmul(ps[g][:, bank, 0:width], gate_bd[:, g, b, :], xc[:, b, t0:t0 + width],
                                       start=True, stop=True)
                    mm.then_inc(ri_summed, 1)

            for s in range(NC + 2):
                def turn(t):
                    if t == 5 and 1 <= s <= NC:
                        turn_probs(s - 1)
                if s == 0:
                    project(5, REAL)
                elif s <= NB:
                    project(5 + s, ALL, turn)
                elif s == NB + 1:
                    lru_gates(0)
                    lru_gates(1)
                    turn(5)
                    lru_gates(2)
                    lru_gates(3)
                else:
                    project(4 + s, REAL, turn, O_BRANCH + s - NB - 2)
                if 1 <= s <= NC:
                    values(s - 1)
                if s < NC:
                    scores(s)

            for u in range(2 * NB):
                attn = u < NB
                head, tail = (ya_head, ya_tail) if attn else (yl_head, yl_tail)

                def ready(t):
                    pe.wait_ge(ya_head_made if attn else yl_head_made, t % NB + 1)
                    pe.wait_ge(ya_tail_made if attn else yl_tail_made, t % NB + 1)
                place = mix_place(O_OUT + u)
                wait_read(pe, place, more=0)
                product(U_OUT + u, ps[place[0]], KD, lambda t: (head[:, t % NB, :], tail[:, t % NB, :]),
                        [(0, 0, SEQ)], before=ready if u % NB == 0 else None, group=NB)
                if u == 0:
                    pe.wait_ge(ya_squared, NC)
                    sum_channels(ps_c[:, 0, :], SEQ, sum_sq[:, N_META:L]).then_inc(norm_summed, 1)
                if u == NB:
                    pe.wait_ge(yl_squared, 1)
                    sum_channels(ps_c[:, 1, :], SEQ, a_sq[:, 0:SEQ]).then_inc(norm_summed, 1)

            ffn(1, REAL)
            norm_sum(3, REAL)

        @block.scalar
        def _(act):
            def split_head(n, i=None):
                cols = unit_tiles(n) * P
                act.wait_ge(w_landed[n % RAW], plus(16 * (n // RAW + 1), i, 16 * SLOTS // RAW))
                if n >= SLOTS:
                    act.wait_ge(units_done, plus(n - SLOTS + 1, i, SLOTS))
                act.activation(w_head[:, n % SLOTS, 0:cols], w_raw[:, n % RAW, 0:cols], ACT.Copy).then_inc(head_made, 1)

            def root(which, src, dst, width):
                act.wait_ge(norm_summed, which)
                act.activation(dst, src, ACT.Sqrt, scale=1.0 / width, bias=eps[:, 0:1]).then_inc(rms_made, 1)

            def ffn(f, pieces):
                cols = span(pieces)

                def four(j, n, i=None):
                    for jj in (j, j + 1):
                        wait_read(act, gu_place(f, 2 * jj), i)
                        act.activation(gate_s[:, cols], gate_s[:, cols], ACT.Silu).then_inc(silu_made, 1)
                        split_head(n + 2 * (jj - j), i)
                        act.wait_ge(hid_made, plus(J * f + jj + 1, i, 2))
                        act.activation(block_of(hid_head, jj, i, 2, cols), up_s[:, cols],
                                       ACT.Copy).then_inc(hid_head_made, 1)
                        split_head(n + 2 * (jj - j) + 1, i)

                root(SUM_FFN1 if f == 0 else SUM_FFN2, banks(ps_c, pieces), by_piece(rstd[:, cols], pieces), D_MODEL)
                with act.Fori(0, TURNS - 1) as i:
                    four(0, U_GU[f] + SLOTS, i)
                four(J - 2, U_DOWN[f])

                def down(m, n, i=None):
                    if n is not None:
                        split_head(n, i)
                    if f == 0:
                        wait_read(act, down_place(f, m), i)
                        gain = vec[:, bass.ds(i * 2 + (VEC["mix"] + m), 1)] if i is not None else col("mix", m)
                        act.activation(block_of(xg_head, m, i, 2), block_of(h, m, i, 2), ACT.Copy,
                                       scale=gain).then_inc(xg_head_made, 1)
                    if n is not None:
                        split_head(n + 1, i)

                with act.Fori(0, 2 * KD // SLOTS - 1) as i:
                    for m in range(2):
                        down(m, U_DOWN[f] + SLOTS + 2 * m, i)
                for m in range(2):
                    down(KD - 2 + m, U_IN + 2 * m if f == 0 else None)

            act.wait_ge(const_made, 1)
            act.wait_ge(vec_landed, 16)
            for k in range(KD):
                if k < 2:
                    split_head(k)
                act.wait_ge(x_landed[k], 16)
                act.activation(xg_head[:, k, :], h[:, k, :], ACT.Copy, scale=col("ffn1", k)).then_inc(xg_head_made, 1)
            for k in range(KD):
                if k >= 2:
                    act.wait_ge(sum_made, k - 1)
                act.activation((gate_s, up_s)[k % 2][:, :], h[:, k, :], ACT.Square).then_inc(square_made, 1)
                if k in (1, 3):
                    split_head(2 + k // 2)
            ffn(0, ALL)

            root(SUM_MIX, banks(ps_c, ALL), by_piece(rstd[:, :], ALL), D_MODEL)
            for u in range(6):
                split_head(U_IN + SLOTS + u)
                if u == 0:
                    act.wait_ge(lru_consts, 1)
                    act.activation(small[:, 1, :], small[:, 0, :], ACT.Exp, scale=-1.0).then_inc(lam_exp, 1)
                if u == 3:
                    act.wait_ge(v_turned, 1)
                    act.activation(v_win[:, 1:NC, :].rearrange("p c d -> p (c d)"),
                                   ps_d[:, :, :].rearrange("p a n -> p (a n)")[:, P:NC * P], ACT.Copy)
                    act.activation(v_meta[:, :], ps_c[0:N_META, 0, 0:P], ACT.Copy).then_inc(v_kept, 1)

            def exps(c):
                act.wait_ge(bias_made, c + 1)
                if c:
                    act.wait_ge(p_turned, c)
                    act.wait_ge(prob_made, c)
                n = keys(c)
                for b in range(NB):
                    act.activation(prob[:, b, 0:n], ps_c[:, b // 2, (b % 2) * KEYS:(b % 2) * KEYS + n], ACT.Exp,
                                   scale=ATTN_SCALE, bias=small[:, 8, b:b + 1], accum_out=small[:, 9, b:b + 1])
                act.activation(small[:, 11, :], small[:, 10, :], ACT.Exp).then_inc(exp_made, 1)

            def keep_probs(c):
                n = keys(c) - N_META
                act.wait_ge(p_turned, c + 1)
                if c:
                    act.wait_ge(pv_made, c)
                act.activation(p_t[0:n, :], ps_d[0:n, 0, :], ACT.Copy).then_inc(p_kept, 1)

            def gate_sigmoids(b):
                for g, dst in ((0, r_a), (1, i_u)):
                    act.wait_ge(ri_summed, 2 * b + g + 1)
                    act.activation(by_piece(dst[:, b, :], ALL), banks(ps[g], ALL), ACT.Sigmoid,
                                   bias=col(("ba", "bx")[g], b)).then_inc(pair_read[g], 1)

            def decay(b):
                act.wait_ge(lru_consts, 2)
                act.activation(one_m_a2[:, b, :], r_a[:, b, :], ACT.Tanh, scale=small[:, 7, b:b + 1])
                act.activation(r_a[:, b, :], r_a[:, b, :], ACT.Exp, scale=small[:, 6, b:b + 1]).then_inc(act_chain, 1)
                act.wait_ge(act_chain, b + 1)
                if b:
                    act.wait_ge(om_made, b)
                act.activation(a_sq[:, :], r_a[:, b, :], ACT.Square).then_inc(a_made, 1)

            for s in range(NC + 1):
                if s and s != NB + 1:
                    split_head(U_IN + 9 + (s if s <= NB else s - 1))
                if s < NC:
                    exps(s)
                if s == NB:
                    gate_sigmoids(0)
                    gate_sigmoids(1)
                if s in (5, 6):
                    decay(2 * (s - 5))
                if s < NC:
                    keep_probs(s)
                if s == NB:
                    gate_sigmoids(2)
                    gate_sigmoids(3)
                if s in (5, 6):
                    decay(2 * (s - 5) + 1)
                if s == 7:
                    for b in range(NB):
                        act.wait_ge(om_made, b + 1)
                        act.activation(one_m_a2[:, b, :], one_m_a2[:, b, :], ACT.Sqrt).then_inc(root_made, 1)

            act.wait_ge(ya_kept, NC)
            for b in range(NB):
                act.activation(ya_head[:, b, :], y_attn[:, b, :], ACT.Copy, scale=col("attn", b)).then_inc(ya_head_made, 1)
            split_head(U_OUT + NB - 1)
            for b in range(NB):
                wait_read(act, mix_place(O_BRANCH + b))
                act.activation(gelu[:, b, :], gelu[:, b, :], ACT.Gelu_apprx_tanh).then_inc(gelu_made, 1)
            act.wait_ge(u_made, 1)
            root(SUM_ATTN, ps_c[:, 0, :], rstd_attn, ATTN_WIDTH)
            for b in range(NB):
                act.wait_ge(yl_made, b + 1)
                act.activation(yl_head[:, b, :], r_a[:, b, 0:SEQ], ACT.Copy, scale=col("lru", b)).then_inc(yl_head_made, 1)
                split_head(U_OUT + NB + b)
            root(SUM_LRU, ps_c[:, 1, :], rstd[:, N_META:L], LRU_WIDTH)
            for u in range(NB):
                split_head(U_GU[1] + u)
                act.wait_ge(h_ready, u + 1)
                for k in (2 * u, 2 * u + 1):
                    act.activation(xg_head[:, k, N_META:L], h[:, k, N_META:L], ACT.Copy,
                                   scale=col("ffn2", k)).then_inc(xg_head_made, 1)
            ffn(1, REAL)
            root(SUM_FINAL, ps_c[:, 0, :], rstd[:, N_META:L], D_MODEL)

        @block.vector
        def _(dve):
            chained = [0]

            def chain(ins):
                chained[0] += 1
                ins.then_inc(dve_chain, 1)
                dve.wait_ge(dve_chain, chained[0])

            def split_tail(n, i=None):
                cols = unit_tiles(n) * P
                dve.wait_ge(head_made, plus(n + 1, i, SLOTS))
                dve.tensor_tensor(w_tail[:, n % SLOTS, 0:cols], w_raw[:, n % RAW, 0:cols],
                                  w_head[:, n % SLOTS, 0:cols].bitcast(F32), ALU.subtract).then_inc(tail_made, 1)

            def tail_of(dst, src, gain, head):
                return dve.scalar_tensor_tensor(out=dst, in0=src, scalar=gain, in1=head.bitcast(F32),
                                                op0=ALU.mult, op1=ALU.subtract)

            def invert(which, ap):
                dve.wait_ge(rms_made, which)
                dve.reciprocal(ap, ap).then_inc(rstd_made, 1)
                dve.wait_ge(rstd_made, which)

            def scaled(place, dst, pieces):
                q = place[0]
                dve.tensor_tensor(by_piece(dst, pieces), banks(ps[q], pieces),
                                  by_piece(rstd[:, span(pieces)], pieces), ALU.mult).then_inc(pair_read[q], 1)

            def ffn(f, pieces):
                cols = span(pieces)

                def four(j, n, i=None):
                    for jj in (j, j + 1):
                        dve.wait_ge(units_done, plus(U_GU[f] + 2 * jj + 1, i, SLOTS))
                        if jj:
                            dve.wait_ge(hid_made, plus(J * f + jj, i, 2))
                        scaled(gu_place(f, 2 * jj), gate_s[:, cols], pieces)
                        split_tail(n + 2 * (jj - j), i)
                        dve.wait_ge(units_done, plus(U_GU[f] + 2 * jj + 2, i, SLOTS))
                        if jj:
                            dve.wait_ge(hid_tail_made, plus(J * f + jj, i, 2))
                        scaled(gu_place(f, 2 * jj + 1), up_s[:, cols], pieces)
                        split_tail(n + 2 * (jj - j) + 1, i)

                invert(SUM_FFN1 if f == 0 else SUM_FFN2, rstd[:, cols])
                four(0, U_GU[f] + SLOTS)
                with dve.Fori(0, TURNS - 2) as i:
                    four(2, U_GU[f] + 2 * SLOTS, i)
                four(J - 2, U_DOWN[f])

                def down(m, n, i=None):
                    if n is not None:
                        split_tail(n, i)
                    dve.wait_ge(units_done, plus(U_DOWN[f] + 2 * m + 2, i, SLOTS))
                    hm = block_of(h, m, i, 2, cols)
                    dve.scalar_tensor_tensor(out=by_piece(hm, pieces), in0=banks(ps[m % 2], pieces), scalar=0.5,
                                             in1=by_piece(hm, pieces), op0=ALU.mult,
                                             op1=ALU.add).then_inc(pair_read[m % 2], 1)
                    if n is not None:
                        split_tail(n + 1, i)
                    if f == 0:
                        wait_read(dve, down_place(f, m), i)
                        dve.wait_ge(xg_head_made, plus(KD + m + 1, i, 2))
                        gain = vec[:, bass.ds(i * 2 + (VEC["mix"] + m), 1)] if i is not None else col("mix", m)
                        tail_of(block_of(xg_tail, m, i, 2), hm, gain, block_of(xg_head, m, i, 2)).then_inc(xg_tail_made, 1)

                with dve.Fori(0, 2 * KD // SLOTS - 1) as i:
                    for m in range(2):
                        down(m, U_DOWN[f] + SLOTS + 2 * m, i)
                for m in range(2):
                    down(KD - 2 + m, U_IN + 2 * m if f == 0 else None)

            dve.wait_ge(vec_landed, 16)
            for k in range(KD):
                if k < 2:
                    split_tail(k)
                dve.wait_ge(x_landed[k], 16)
                dve.wait_ge(xg_head_made, k + 1)
                tail_of(xg_tail[:, k, :], h[:, k, :], col("ffn1", k), xg_head[:, k, :]).then_inc(xg_tail_made, 1)
            split_tail(2)
            split_tail(3)
            ffn(0, ALL)

            def vcols(name):
                return vec[:, VEC[name]:VEC[name] + NB]

            def lru_exponents():
                lam, s = vcols("lam"), small
                chain(dve.tensor_scalar(s[:, 2, :], lam, -1.0, None, ALU.mult))
                dve.tensor_tensor(s[:, 0, :], lam, s[:, 2, :], ALU.max).then_inc(lru_consts, 1)
                dve.wait_ge(lam_exp, 1)
                chain(dve.tensor_scalar(s[:, 2, :], s[:, 1, :], 2.0, None, ALU.add))
                chain(dve.reciprocal(s[:, 3, :], s[:, 2, :]))
                chain(dve.tensor_tensor(s[:, 2, :], s[:, 1, :], s[:, 3, :], ALU.mult))
                chain(dve.tensor_tensor(s[:, 3, :], s[:, 2, :], s[:, 2, :], ALU.mult))
                chain(dve.tensor_scalar(s[:, 4, :], s[:, 3, :], 1.0 / 17.0, None, ALU.mult))
                for n in range(15, 1, -2):
                    chain(dve.scalar_tensor_tensor(out=s[:, 4, :], in0=s[:, 4, :], scalar=1.0 / n, in1=s[:, 3, :],
                                                   op0=ALU.add, op1=ALU.mult))
                chain(dve.scalar_tensor_tensor(out=s[:, 4, :], in0=s[:, 4, :], scalar=1.0, in1=s[:, 2, :],
                                               op0=ALU.add, op1=ALU.mult))
                chain(dve.tensor_scalar(s[:, 5, :], lam, -1.0, 0.0, ALU.mult, ALU.max))
                chain(dve.scalar_tensor_tensor(out=s[:, 5, :], in0=s[:, 4, :], scalar=2.0, in1=s[:, 5, :],
                                               op0=ALU.mult, op1=ALU.add))
                dve.tensor_scalar(s[:, 6, :], s[:, 5, :], -LRU_C, None, ALU.mult)
                dve.tensor_scalar(s[:, 7, :], s[:, 5, :], LRU_C, None, ALU.mult).then_inc(lru_consts, 1)
                chain(dve.tensor_scalar(s[:, 12, :], vcols("sink"), -1.0, None, ALU.mult))

            dve.wait_ge(units_done, U_IN)
            invert(SUM_MIX, rstd[:, :])

            def project(u, dst, pieces, o=None):
                dve.wait_ge(units_done, U_IN + u + 1)
                scaled(mix_place(u if o is None else o), dst, pieces)

            project(0, k_t[:, :], ALL)
            split_tail(U_IN + SLOTS)
            lru_exponents()
            project(1, v_t[:, :], ALL)
            split_tail(U_IN + SLOTS + 1)
            w = NC - 1
            chunks = k_t[:, N_META:L].rearrange("p (w n) -> p w n", w=NC)
            dve.tensor_copy(k_win[:, 1:NC, N_META:N_META + CHUNK], chunks[:, 0:w, :])
            dve.tensor_copy(k_win[:, 1:NC, N_META + CHUNK:KEYS], chunks[:, 1:NC, :])
            dve.tensor_copy(k_win[:, 1:NC, 0:N_META],
                            k_t[:, 0:N_META].unsqueeze(1).broadcast_to([P, w, N_META])).then_inc(k_windows, 1)
            for u in range(2, 6):
                project(u, q_t[:, u - 2, :], REAL)
                split_tail(U_IN + SLOTS + u)

            def softmax_bias(c):
                dve.wait_ge(scores_made, c + 1)
                chain(dve.tensor_reduce(small[:, 13, :].rearrange("p (a b) -> p a b", a=2),
                                        ps_c[:, :, 0:2 * KEYS].rearrange("p a (b n) -> p a b n", b=2)[:, :, :, 0:keys(c)],
                                        AX_X, ALU.max))
                chain(dve.scalar_tensor_tensor(out=small[:, 8, :], in0=small[:, 13, :], scalar=-ATTN_SCALE,
                                               in1=small[:, 12, :], op0=ALU.mult, op1=ALU.min))
                dve.tensor_tensor(small[:, 10, :], vcols("sink"), small[:, 8, :], ALU.add).then_inc(bias_made, 1)

            def softmax_scale(c):
                n = keys(c)
                dve.wait_ge(exp_made, c + 1)
                chain(dve.tensor_tensor(small[:, 14, :], small[:, 9, :], small[:, 11, :], ALU.add))
                chain(dve.reciprocal(small[:, 15, :], small[:, 14, :]))
                dve.tensor_tensor(prob[:, :, 0:n], prob[:, :, 0:n],
                                  small[:, 15, :].unsqueeze(2).broadcast_to([P, NB, n]),
                                  ALU.mult).then_inc(prob_made, 1)

            def keep_meta_probs(c):
                dve.wait_ge(p_turned, c + 1)
                if c:
                    dve.wait_ge(pv_made, c)
                dve.tensor_copy(p_t_meta[:, :], ps_d[0:N_META, 1, :]).then_inc(pm_kept, 1)

            def keep_values(c):
                dve.wait_ge(pv_made, c + 1)
                dve.tensor_copy(y_attn[:, :, c * CHUNK:(c + 1) * CHUNK],
                                ps_d[:, 1, 0:NB * CHUNK].rearrange("p (b q) -> p b q", b=NB)).then_inc(ya_kept, 1)

            def conv_tap(b, tap):
                last = CONV_WIDTH - 1
                weight = col("conv_w", tap * NB + b)
                if tap == last:
                    wait_read(dve, mix_place(O_X + b))
                    dve.wait_ge(mixer_const, 3)
                    chain(dve.tensor_scalar(xc[:, b, :], x_pad[:, last:last + L], weight, col("conv_b", b),
                                            ALU.mult, ALU.add))
                    return
                ins = dve.scalar_tensor_tensor(out=xc[:, b, :], in0=x_pad[:, tap:tap + L], scalar=weight,
                                               in1=xc[:, b, :], op0=ALU.mult, op1=ALU.add)
                if tap:
                    chain(ins)
                else:
                    ins.then_inc(conv_made, 1)

            def one_less_a_squared(b):
                dve.wait_ge(a_made, b + 1)
                dve.scalar_tensor_tensor(out=one_m_a2[:, b, :], in0=a_sq[:, :], scalar=1.0,
                                         in1=one_m_a2[:, b, :], op0=ALU.add, op1=ALU.mult).then_inc(om_made, 1)

            def states(b):
                dve.wait_ge(u_made, b + 1)
                chain(dve.tensor_tensor_scan(xc[:, b, :], r_a[:, b, :], i_u[:, b, :], 0.0, ALU.mult, ALU.add))

            for s in range(NC + 1):
                conv = s - 1 if 1 <= s <= NB else None
                if s < NC:
                    softmax_bias(s)
                if s and s != NB + 1:
                    split_tail(U_IN + 9 + (s if s <= NB else s - 1))
                if conv is not None:
                    conv_tap(conv, 3)
                if s < NC:
                    softmax_scale(s)
                if conv is not None:
                    conv_tap(conv, 2)
                if s in (5, 6):
                    one_less_a_squared(2 * (s - 5))
                if s < NC:
                    keep_meta_probs(s)
                if conv is not None:
                    conv_tap(conv, 1)
                if s == NB:
                    conv_tap(conv, 0)
                if s < NC:
                    keep_values(s)
                if conv is not None and s < NB:
                    conv_tap(conv, 0)
                if s in (5, 6):
                    one_less_a_squared(2 * (s - 5) + 1)
                if s == 8:
                    for b in range(NB):
                        dve.wait_ge(ya_head_made, b + 1)
                        tail_of(ya_tail[:, b, :], y_attn[:, b, :], col("attn", b), ya_head[:, b, :]).then_inc(ya_tail_made, 1)
                if s < NB:
                    if s:
                        dve.wait_ge(conv_made, s)
                    project(6 + s, x_pad[:, CONV_WIDTH - 1:], ALL)
                elif s > NB:
                    b = s - NB - 1
                    project(10 + b, gelu[:, b, :], REAL, O_BRANCH + b)
            split_tail(U_OUT + NB - 1)

            def out_step(u, factor):
                dve.wait_ge(units_done, U_OUT + u + 1)
                if u:
                    dve.wait_ge(h_attn if u <= NB else h_ready, u if u <= NB else u - NB)
                place = mix_place(O_OUT + u)
                dve.tensor_tensor(y_scaled[:, :, :], ps[place[0]][:, :, :],
                                  factor.unsqueeze(1).broadcast_to([P, 2, SEQ]), ALU.mult).then_inc(pair_read[place[0]], 1)
                wait_read(dve, place)
                k = 2 * (u % NB)
                ins = dve.tensor_tensor(h[:, k:k + 2, N_META:L], h[:, k:k + 2, N_META:L], y_scaled[:, :, :], ALU.add)
                ins.then_inc(h_ready if u >= NB else h_attn, 1)

            def gated(b):
                states(b)
                dve.wait_ge(gelu_made, b + 1)
                dve.tensor_tensor(r_a[:, b, 0:SEQ], gelu[:, b, :], xc[:, b, N_META:L], ALU.mult).then_inc(yl_made, 1)

            for b in range(NB):
                gated(b)
            invert(SUM_ATTN, rstd_attn)
            for b in range(NB):
                out_step(b, rstd_attn)
                dve.wait_ge(yl_head_made, b + 1)
                tail_of(yl_tail[:, b, :], r_a[:, b, 0:SEQ], col("lru", b), yl_head[:, b, :]).then_inc(yl_tail_made, 1)
                split_tail(U_OUT + NB + b)
            invert(SUM_LRU, rstd[:, N_META:L])
            for u in range(NB):
                dve.wait_ge(h_attn, NB)
                out_step(NB + u, rstd[:, N_META:L])
                split_tail(U_GU[1] + u)
                dve.wait_ge(h_ready, u + 1)
                for k in (2 * u, 2 * u + 1):
                    dve.wait_ge(xg_head_made, 2 * KD + k + 1)
                    tail_of(xg_tail[:, k, N_META:L], h[:, k, N_META:L], col("ffn2", k),
                            xg_head[:, k, N_META:L]).then_inc(xg_tail_made, 1)
            ffn(1, REAL)

            invert(SUM_FINAL, rstd[:, N_META:L])
            for m in range(KD):
                dve.scalar_tensor_tensor(out=h[:, m, N_META:L], in0=h[:, m, N_META:L], scalar=col("final", m),
                                         in1=rstd[:, N_META:L], op0=ALU.mult, op1=ALU.mult).then_inc(out_made, 1)

        @block.gpsimd
        def _(pool):
            chained = [0]

            def chain(ins):
                chained[0] += 1
                ins.then_inc(pool_chain, 1)
                pool.wait_ge(pool_chain, chained[0])

            def identity():
                chain(pool.memset(ident[:, :], 0.0))
                pool.affine_select(out=ident[:, :], in_=ident[:, :], compare_op=ALU.not_equal, fill=1.0, base=0,
                                   pattern=[[-1, P]], channel_multiplier=1).then_inc(mixer_const, 1)

            def clear_sum(which):
                if which > 1:
                    pool.wait_ge(norm_summed, which - 1)
                pool.memset(sum_sq[:, :], 0.0).then_inc(sum_zero, 1)
                pool.wait_ge(sum_zero, {SUM_FFN1: 1, SUM_MIX: 2, SUM_FFN2: 3, SUM_FINAL: 4}[which])

            def add_square(v, k, cols, i=None):
                hk = block_of(h, k, i, 2, cols)
                pool.tensor_tensor(square[:, cols], hk, hk, ALU.mult).then_inc(square_made, 1)
                pool.wait_ge(square_made, plus(KD * v + k + 1, i, 2))
                pool.tensor_tensor(sum_sq[:, cols], sum_sq[:, cols], square[:, cols], ALU.add).then_inc(sum_made, 1)
                pool.wait_ge(sum_made, plus(KD * v + k + 1, i, 2))

            def ffn(f, pieces):
                cols = span(pieces)
                with pool.Fori(0, J // 2) as i:
                    for j in range(2):
                        pool.wait_ge(silu_made, plus(J * f + j + 1, i, 2))
                        wait_read(pool, gu_place(f, 2 * j + 1), i)
                        pool.tensor_tensor(up_s[:, cols], gate_s[:, cols], up_s[:, cols], ALU.mult).then_inc(hid_made, 1)
                        pool.wait_ge(hid_head_made, plus(J * f + j + 1, i, 2))
                        pool.tensor_tensor(block_of(hid_tail, j, i, 2, cols), up_s[:, cols],
                                           block_of(hid_head, j, i, 2, cols).bitcast(F32),
                                           ALU.subtract).then_inc(hid_tail_made, 1)
                v = 2 * f + 1
                clear_sum(SUM_MIX if f == 0 else SUM_FINAL)
                with pool.Fori(0, KD // 2) as i:
                    for m in range(2):
                        wait_read(pool, down_place(f, m), i)
                        add_square(v, m, cols, i)

            pool.memset(ones[:, :], 1.0)
            pool.memset(eps[:, :], EPS).then_inc(const_made, 1)
            clear_sum(SUM_FFN1)
            for k in range(KD):
                pool.wait_ge(square_made, k + 1)
                pool.tensor_tensor(sum_sq[:, :], sum_sq[:, :], (gate_s, up_s)[k % 2][:, :], ALU.add).then_inc(sum_made, 1)
                pool.wait_ge(sum_made, k + 1)
            ffn(0, ALL)

            pool.wait_ge(units_done, U_IN)
            pool.memset(gate_bd[:, :, :, :], 0.0).then_inc(mixer_const, 1)
            identity()
            pool.memset(x_pad[:, 0:CONV_WIDTH - 1], 0.0).then_inc(mixer_const, 1)

            pool.wait_ge(norm_summed, SUM_MIX)
            for c in range(NC):
                if c == 5:
                    for b in range(NB):
                        wait_read(pool, mix_place(O_GATE + 2 * b + 1))
                        pool.wait_ge(conv_made, b + 1)
                        pool.tensor_tensor(i_u[:, b, :], i_u[:, b, :], xc[:, b, :], ALU.mult).then_inc(ix_made, 1)
                t0 = c * CHUNK
                pool.wait_ge(ya_kept, c + 1)
                sq = square[:, 0:NB * CHUNK].rearrange("p (b q) -> p b q", b=NB)
                two = square[:, NB * CHUNK:NB * CHUNK + 2 * CHUNK].rearrange("p (b q) -> p b q", b=2)
                yc = y_attn[:, :, t0:t0 + CHUNK]
                chain(pool.tensor_tensor(sq, yc, yc, ALU.mult))
                chain(pool.tensor_tensor(two, sq[:, 0:2, :], sq[:, 2:4, :], ALU.add))
                pool.tensor_tensor(sum_sq[:, N_META + t0:N_META + t0 + CHUNK], two[:, 0, :], two[:, 1, :],
                                   ALU.add).then_inc(ya_squared, 1)
            for b in range(NB):
                pool.wait_ge(ix_made, b + 1)
                pool.wait_ge(root_made, b + 1)
                pool.tensor_tensor(i_u[:, b, :], i_u[:, b, :], one_m_a2[:, b, :], ALU.mult).then_inc(u_made, 1)
            lru_sum = a_sq[:, 0:SEQ]
            for b in range(NB):
                pool.wait_ge(yl_made, b + 1)
                yb = r_a[:, b, 0:SEQ]
                if b == 0:
                    ins = pool.tensor_tensor(lru_sum, yb, yb, ALU.mult)
                else:
                    chain(pool.tensor_tensor(square[:, 0:SEQ], yb, yb, ALU.mult))
                    ins = pool.tensor_tensor(lru_sum, lru_sum, square[:, 0:SEQ], ALU.add)
                if b < NB - 1:
                    chain(ins)
                else:
                    ins.then_inc(yl_squared, 1)

            clear_sum(SUM_FFN2)
            for k in range(KD):
                pool.wait_ge(h_ready, k // 2 + 1)
                add_square(2, k, slice(N_META, L))
            ffn(1, REAL)


def kernel(x, meta_tokens, ffn1_norm, ffn1_w_gate, ffn1_w_up, ffn1_w_down, mix_norm, w_in, attn_sinks, conv_w, conv_b,
           lru_wa, lru_ba, lru_wx, lru_bx, lru_lambda, attn_out_norm, lru_out_norm, w_out, ffn2_norm, ffn2_w_gate,
           ffn2_w_up, ffn2_w_down, final_norm):
    import numpy as np

    import concourse.bacc as bacc
    from concourse.bass_utils import run_bass_kernel_spmd

    def tiles(w, rows, cols):
        return np.asarray(w).reshape(rows, P, cols, P).transpose(0, 2, 1, 3)

    def units(t):
        return np.ascontiguousarray(t.transpose(0, 2, 1, 3).reshape(t.shape[0], P, t.shape[1] * P))

    def gate_up(gate, up):
        both = np.stack([tiles(gate[0], KD, J), tiles(up[0], KD, J)])
        return units(both.transpose(2, 0, 1, 3, 4).reshape(2 * J, KD, P, P))

    def down(w):
        t = tiles(w[0], J, KD).reshape(2, HJ, KD, P, P)
        return units(t.transpose(2, 0, 1, 3, 4).reshape(2 * KD, HJ, P, P))

    def columns(a):
        return np.asarray(a).reshape(-1, P).T

    heads = np.arange(ATTN_WIDTH).reshape(2, NB, HEAD_DIM).transpose(1, 0, 2).reshape(-1)
    w = np.asarray(w_in[0])
    q, k, v, x_lru, branch = np.split(w, np.cumsum([ATTN_WIDTH, P, P, LRU_WIDTH]), axis=1)
    w_in_units = units(tiles(np.concatenate([k, v, q[:, heads], x_lru, branch], axis=1), KD, U_OUT - U_IN)
                       .transpose(1, 0, 2, 3))
    w = np.asarray(w_out[0])
    w = np.concatenate([w[0:ATTN_WIDTH][heads], w[ATTN_WIDTH:]])
    t = tiles(w, 2 * NB, KD).reshape(2, NB, KD // 2, 2, P, P)
    w_out_units = units(t.transpose(0, 2, 3, 1, 4, 5).reshape(2 * NB, KD, P, P))

    def gates(a):
        return np.asarray(a[0]).reshape(NB, P, 64).transpose(1, 0, 2)

    sinks = np.repeat(np.asarray(attn_sinks[0]).reshape(2, NB), 64, axis=0)
    vecs = np.concatenate([columns(a) for a in (
        ffn1_norm[0], mix_norm[0], ffn2_norm[0], final_norm, attn_out_norm[0][heads], lru_out_norm[0], conv_w[0],
        conv_b[0], lru_ba[0], lru_bx[0], lru_lambda[0])] + [sinks], axis=1)
    tokens = np.concatenate([np.asarray(meta_tokens), np.asarray(x[0])])
    arrays = {
        "x_t": tokens.T.reshape(KD, P, L),
        "ffn1_gu": gate_up(ffn1_w_gate, ffn1_w_up), "ffn1_down": down(ffn1_w_down),
        "w_in": w_in_units, "w_out": w_out_units,
        "ffn2_gu": gate_up(ffn2_w_gate, ffn2_w_up), "ffn2_down": down(ffn2_w_down),
        "gate_w": np.stack([gates(lru_wa), gates(lru_wx)], axis=1),
        "vecs": vecs,
    }
    arrays = {name: np.ascontiguousarray(a) for name, a in arrays.items()}
    nc = bacc.Bacc("TRN2", target_bir_lowering=False, num_devices=1)
    args = {name: nc.dram_tensor(name, a.shape, mybir.dt.from_np(a.dtype), kind="ExternalInput").ap()
            for name, a in arrays.items()}
    args["out_t"] = nc.dram_tensor("out_t", (KD, P, SEQ), F32, kind="ExternalOutput").ap()
    build_layer(nc, **args)
    r = run_bass_kernel_spmd(nc, [arrays], core_ids=[0])
    out = r.results[0]["out_t"]
    return np.ascontiguousarray(out.reshape(D_MODEL, SEQ).T)[None]
```

```python
import math
from contextlib import ExitStack

import concourse.bass as bass
from concourse import mybir

F32 = mybir.dt.float32
F32R = mybir.dt.float32r
ALU = mybir.AluOpType
ACT = mybir.ActivationFunctionType
AX_X = mybir.AxisListType.X

P = 128
D_MODEL, SEQ, N_META, D_FF = 1024, 512, 16, 2816
CHUNK, HEAD_DIM, LRU_WIDTH, CONV_WIDTH = 64, 64, 512, 4
EPS, LRU_C = 1e-6, 8.0
ATTN_SCALE = HEAD_DIM ** -0.5
L = N_META + SEQ
KD = D_MODEL // P
J = D_FF // P
HJ = J // 2
NB = LRU_WIDTH // P
NC = SEQ // CHUNK
KEYS = N_META + 2 * CHUNK
ATTN_WIDTH = NB * P
SLOTS, RAW = 4, 2
HALF = KD // 2 * P

U_GU = (0, 82)
U_DOWN = (44, 126)
U_IN, U_OUT = 60, 74
U_Q, U_V, U_X, U_BRANCH = U_IN + 1, U_IN + 1 + NB, U_IN + 2 + NB, U_IN + 2 + 2 * NB

GATES_IN = U_X + 2
TURNS = 2 * J // SLOTS

MIX_PLACE, _reads = {}, [TURNS + KD // 2] * 2
for _u in range(U_IN, U_OUT):
    _q = _u % 2
    MIX_PLACE[_u] = _q, _reads[_q]
    _reads[_q] += 1
    if 0 <= _u - GATES_IN < NB:
        for _g in range(2):
            MIX_PLACE[_g, _u - GATES_IN] = 1 - _q, _reads[1 - _q]
            _reads[1 - _q] += 1
OUT_PAIRS = (0, 1, 3)
READS_OUT = (_reads[0], _reads[1], TURNS, TURNS)
READS_FFN2 = tuple(READS_OUT[q] + (len(range(OUT_PAIRS.index(q), 2 * NB, 3)) if q in OUT_PAIRS else 0)
                   for q in range(4))

ALL = [(0, 0, L // 2), (1, L // 2, L // 2)]
REAL = [(0, N_META, SEQ)]

POOL_OUT, DVE_OUT = (0, 1), (2, 3, 4, 5, 6, 7)
OUT_ORDER = (2, 3, 4, 5, 0, 6, 7, 1)
TB = SEQ // P

VEC = {}
_at = 0
for _name, _n in (("ffn1", KD), ("mix", KD), ("ffn2", KD), ("final", KD), ("attn", NB), ("lru", NB),
                  ("conv_w", CONV_WIDTH * NB), ("conv_b", NB), ("ba", NB), ("bx", NB), ("lam", NB), ("sink", NB)):
    VEC[_name] = _at
    _at += _n
NVEC = _at


def keys(c):
    return KEYS if c else KEYS - CHUNK


def build_layer(nc, x_t, ffn1_gu, ffn1_down, w_in, w_out, ffn2_gu, ffn2_down, gate_w, vecs, out_t):
    with ExitStack() as ctx:
        def sb(name, shape, dt=F32, where=ctx):
            return where.enter_context(nc.sbuf_tensor(name, shape, dt))

        def sem(name):
            return ctx.enter_context(nc.semaphore(name))

        h = sb("h", [P, KD, L])
        xg_head = sb("xg_head", [P, KD, L], F32R)
        xg_tail = sb("xg_tail", [P, KD, L], F32R)
        w_raw = sb("w_raw", [P, RAW, HJ * P])
        w_head = sb("w_head", [P, SLOTS, HJ * P], F32R)
        w_tail = sb("w_tail", [P, SLOTS, HJ * P], F32R)
        rstd = sb("rstd", [P, L])
        square = sb("square", [P, L])
        sum_sq = sb("sum_sq", [P, L])
        ones = sb("ones", [P, P])
        vec = sb("vec", [P, NVEC])
        eps = sb("eps", [P, 1])
        table_out = sb("table_out", [P, 1])

        with ExitStack() as ffn:
            hid_head = sb("hid_head", [P, J, L], F32R, ffn)
            hid_tail = sb("hid_tail", [P, J, L], F32R, ffn)
            gate_s = sb("gate_s", [P, L], F32, ffn)
            up_s = sb("up_s", [P, L], F32, ffn)
        with ExitStack() as early:
            q_t = sb("q_t", [P, NB, SEQ], F32, early)
            k_win = sb("k_win", [P, NC, KEYS], F32, early)
        ya_head = sb("ya_head", [P, NB, SEQ], F32R)
        ya_tail = sb("ya_tail", [P, NB, SEQ], F32R)
        with ExitStack() as early:
            k_t = sb("k_t", [P, L], F32, early)
            v_t = sb("v_t", [P, L], F32, early)
        one_m_a2 = sb("one_m_a2", [P, NB, L])
        with ExitStack() as early:
            p_t = sb("p_t", [P, NB * P], F32, early)
            p_t_meta = sb("p_t_meta", [N_META, NB * P], F32, early)
        y_scaled_even = sb("y_scaled_even", [P, 2, SEQ])
        with ExitStack() as early:
            gelu = sb("gelu", [P, NB, SEQ], F32, early)
        yl_tail = sb("yl_tail", [P, NB, SEQ], F32R)
        yl_head = sb("yl_head", [P, NB, SEQ], F32R)
        v_win = sb("v_win", [P, NC, P])
        v_meta = sb("v_meta", [N_META, P])
        prob = sb("prob", [P, NB, KEYS])
        y_attn = sb("y_attn", [P, NB, SEQ])
        x_pad = sb("x_pad", [P, CONV_WIDTH - 1 + L])
        xc = sb("xc", [P, NB, L])
        r_a = sb("r_a", [P, NB, L])
        i_u = sb("i_u", [P, NB, L])
        a_sq = sb("a_sq", [P, L])
        gate_bd = sb("gate_bd", [P, 2, NB, P])
        ident = sb("ident", [P, P])
        small = sb("small", [P, 16, NB])
        rms_tok = {}
        diagonal = prob[:, :, :].rearrange("p b n -> p (b n)")[:, 0:SEQ]
        last_chunk_sq = y_attn[:, 0, :]

        ps = [ctx.enter_context(nc.psum_tensor(f"ps{i}", [P, 2, 512], F32)) for i in range(4)]
        ps_c, ps_d = ps[2], ps[3]
        token_sum = ps_c[:, 0, 0:64 * TB]
        y_scaled = (y_scaled_even[:, :, :], v_win[:, :, :].rearrange("p (a c) d -> p a (c d)", a=2))
        rstd_attn = x_pad[:, 0:SEQ]
        rstd_lru = rstd[:, N_META:L]

        x_landed = [sem(f"x_landed{k}") for k in range(KD)]
        vec_landed, bd_landed = sem("vec_landed"), sem("bd_landed")
        w_landed = [sem(f"w_landed{r}") for r in range(RAW)]
        half_landed, half_head, half_tail = sem("half_landed"), sem("half_head"), sem("half_tail")
        head_made, tail_made = sem("head_made"), sem("tail_made")
        units_done = sem("units_done")
        pair_read = [sem(f"pair_read{q}") for q in range(4)]
        const_made, mixer_const = sem("const_made"), sem("mixer_const")
        h_ready, xg_head_made, xg_tail_made = sem("h_ready"), sem("xg_head_made"), sem("xg_tail_made")
        sum_zero, square_made, sum_made = sem("sum_zero"), sem("square_made"), sem("sum_made")
        norm_summed, rms_made, rstd_made = sem("norm_summed"), sem("rms_made"), sem("rstd_made")
        silu_made, hid_made = sem("silu_made"), sem("hid_made")
        hid_head_made, hid_tail_made = sem("hid_head_made"), sem("hid_tail_made")
        dve_chain = sem("dve_chain")
        pool_chain = sem("pool_chain")
        lru_consts, lam_exp = sem("lru_consts"), sem("lam_exp")
        k_windows, v_turned, v_kept = sem("k_windows"), sem("v_turned"), sem("v_kept")
        scores_made, bias_made = sem("scores_made"), sem("bias_made")
        exp_made, prob_made = sem("exp_made"), sem("prob_made")
        p_turned, p_kept, pm_kept = sem("p_turned"), sem("p_kept"), sem("pm_kept")
        pv_made, ya_kept, ya_squared = sem("pv_made"), sem("ya_kept"), sem("ya_squared")
        conv_made, gate_ready, ix_made = sem("conv_made"), sem("gate_ready"), sem("ix_made")
        decay_made = sem("decay_made")
        a_sq_made, om_made, root_made, u_made = sem("a_sq_made"), sem("om_made"), sem("root_made"), sem("u_made")
        gelu_made = sem("gelu_made")
        gates_made = sem("gates_made")
        yl_made, yl_squared, lru_summed = sem("yl_made"), sem("yl_squared"), sem("lru_summed")
        ya_head_made, ya_tail_made = sem("ya_head_made"), sem("ya_tail_made")
        yl_head_made, yl_tail_made = sem("yl_head_made"), sem("yl_tail_made")
        h_attn = sem("h_attn")
        last_square, identity_again, diagonal_made = sem("last_square"), sem("identity_again"), sem("diagonal_made")
        rstd_spread, rstd_kept, gained = sem("rstd_spread"), sem("rstd_kept"), sem("gained")
        out_made, pool_out_made, stored = sem("out_made"), sem("pool_out_made"), sem("stored")

        def unit_tiles(n):
            return HJ if (U_DOWN[0] <= n < U_IN or n >= U_DOWN[1]) else KD

        def col(name, i):
            return vec[:, VEC[name] + i:VEC[name] + i + 1]

        def plus(n, i, per):
            return n if i is None else i * per + n

        def block_of(t, k, i=None, per=0, cols=slice(0, L)):
            if i is None:
                return t[:, k, cols]
            return t[:, bass.ds(i * per + k, 1), cols].rearrange("p a n -> p (a n)")

        def by_piece(ap, pieces):
            return ap.rearrange("p (a n) -> p a n", a=len(pieces))

        def banks(pr, pieces):
            return pr[:, 0:len(pieces), 0:pieces[0][2]]

        def span(pieces):
            return slice(pieces[0][1], L)

        def gu_place(f, u):
            q = (0, 1, 3, 2)[u % SLOTS]
            return q, (0, READS_FFN2[q])[f] + u // SLOTS

        def down_place(f, m):
            return m % 2, (0, READS_FFN2[m % 2])[f] + TURNS + m // 2

        def out_place(u):
            q = OUT_PAIRS[u % 3]
            return q, READS_OUT[q] + u // 3

        def wait_read(eng, place, i=None, more=1):
            q, before = place
            if before + more > 0:
                eng.wait_ge(pair_read[q], plus(before + more, i, 1))

        SUM_FFN1, SUM_MIX, SUM_ATTN, SUM_LRU, SUM_FFN2, SUM_FINAL = range(1, 7)
        for n, which in enumerate((SUM_ATTN, SUM_LRU, SUM_FINAL)):
            rms_tok[which] = small[:, n, :]
        block = ctx.enter_context(nc.Block())

        @block.sync
        def _(sp):
            def load(n, src, i=None):
                if n >= RAW:
                    sp.wait_ge(head_made, plus(n - RAW + 1, i, SLOTS))
                    sp.wait_ge(tail_made, plus(n - RAW + 1, i, SLOTS))
                if n == RAW:
                    sp.wait_ge(half_head, 1)
                    sp.wait_ge(half_tail, 1)
                sp.dma_start(w_raw[:, n % RAW, 0:unit_tiles(n) * P], src).then_inc(w_landed[n % RAW], 16)

            def sweep(first, u, turns, dram):
                with sp.Fori(0, turns) as i:
                    for s in range(SLOTS):
                        load(first + s, dram[bass.ds(i * SLOTS + (u + s), 1), :, :].rearrange("a p n -> (a p) n"), i)

            sp.dma_start(vec[:, :], vecs).then_inc(vec_landed, 16)
            sp.dma_start(h[:, 0, :], x_t[0, :, :]).then_inc(x_landed[0], 16)
            sp.dma_start(w_raw[:, 0, 0:HALF], ffn1_gu[0, :, 0:HALF]).then_inc(half_landed, 16)
            sp.dma_start(w_raw[:, 0, HALF:KD * P], ffn1_gu[0, :, HALF:KD * P]).then_inc(w_landed[0], 16)
            for k in range(1, KD):
                sp.dma_start(h[:, k, :], x_t[k, :, :]).then_inc(x_landed[k], 16)
            for u in range(1, SLOTS):
                load(u, ffn1_gu[u, :, :])
            sweep(SLOTS, SLOTS, 2 * J // SLOTS - 1, ffn1_gu)
            sweep(U_DOWN[0], 0, 2 * KD // SLOTS, ffn1_down)
            for u in range(SLOTS):
                load(U_IN + u, w_in[u, :, :])
            sp.wait_ge(mixer_const, 1)
            for half in (slice(0, 64), slice(64, P)):
                for g in range(2):
                    sp.dma_start(gate_bd[half, g, :, half], gate_w[half, g, :, :]).then_inc(bd_landed, 16)
            for u in range(SLOTS, U_OUT - U_IN):
                load(U_IN + u, w_in[u, :, :])
            for u in range(U_GU[1] - U_OUT):
                load(U_OUT + u, w_out[u, :, :])
            sweep(U_GU[1], 0, 2 * J // SLOTS, ffn2_gu)
            sweep(U_DOWN[1], 0, 2 * KD // SLOTS, ffn2_down)
            for m in OUT_ORDER:
                if m in POOL_OUT:
                    sp.wait_ge(pool_out_made, POOL_OUT.index(m) + 1)
                else:
                    sp.wait_ge(out_made, DVE_OUT.index(m) + 1)
                sp.dma_start(out_t[m, :, :], h[:, m, N_META:L]).then_inc(stored, 16)
            sp.wait_ge(stored, 16 * KD)

        @block.tensor
        def _(pe):
            def product(n, pr, tiles, rhs, pieces, i=None, start=True, stop=True, before=None, group=None):
                if n:
                    pe.wait_ge(head_made, plus(n + 1, i, SLOTS))
                    pe.wait_ge(tail_made, plus(n + 1, i, SLOTS))
                s = n % SLOTS
                group = group or tiles
                for t in range(tiles):
                    if n == 0 and t in (0, KD // 2):
                        pe.wait_ge(half_head if t == 0 else head_made, 1)
                        pe.wait_ge(half_tail if t == 0 else tail_made, 1)
                    if before is not None:
                        before(t)
                    head, tail = rhs(t)
                    w_h, w_t = w_head[:, s, t * P:(t + 1) * P], w_tail[:, s, t * P:(t + 1) * P]
                    for p, (w, x) in enumerate(((w_h, head), (w_h, tail), (w_t, head))):
                        for bank, t0, width in pieces:
                            mm = pe.matmul(pr[:, bank + t // group, 0:width], w, x[:, t0:t0 + width],
                                           start=start and p == 0 and t % group == 0,
                                           stop=stop and p == 2 and t % group == group - 1)
                mm.then_inc(units_done, 1)

            def sum_channels(dst, width, ap):
                return pe.matmul(dst[:, 0:width], ones[:, :], ap, start=True, stop=True)

            def norm_sum(v, pieces):
                pe.wait_ge(sum_made, KD * (v + 1) - 1)
                for bank, t0, width in pieces:
                    mm = sum_channels(ps_c[:, bank, :], width, sum_sq[:, t0:t0 + width])
                mm.then_inc(norm_summed, 1)

            def token_sums(squares, first=True, last=True):
                for b in range(TB):
                    mm = pe.matmul(token_sum[:, 64 * b:64 * b + 64], squares[:, b * P:(b + 1) * P], ones[:, 0:64],
                                   start=first and b == 0, stop=last and b == TB - 1, skip_group_check=True)
                return mm

            def spread_rstd(n, dst):
                for b in range(TB):
                    pe.wait_ge(diagonal_made, TB * n + b + 1)
                    cols = slice(b * P, (b + 1) * P)
                    mm = pe.matmul(dst[:, cols], ones[:, :], diagonal[:, cols], start=True, stop=True)
                return mm

            def xg(t):
                return xg_head[:, t, :], xg_tail[:, t, :]

            def xg_ready(v):
                def before(t):
                    pe.wait_ge(xg_head_made, KD * v + t + 1)
                    pe.wait_ge(xg_tail_made, KD * v + t + 1)
                return before

            def ffn(f, pieces):
                v = 2 * f

                def sum_within(t):
                    if t == 2:
                        norm_sum(v, pieces)

                def four(u, i=None):
                    first = i is None
                    for s in range(SLOTS):
                        place = gu_place(f, u + s)
                        if first and s == SLOTS - 1:
                            pe.wait_ge(rms_made, SUM_FFN1 if f == 0 else SUM_FFN2)
                        wait_read(pe, place, i, more=0)
                        product(U_GU[f] + u + s, ps[place[0]], KD, xg, pieces, i,
                                before=(xg_ready(v) if s == 0 else sum_within if s == 2 else None) if first else None)

                four(0)
                with pe.Fori(0, TURNS - 1) as i:
                    four(SLOTS, i)

                def hid(part):
                    return lambda t: (hid_head[:, part * HJ + t, :], hid_tail[:, part * HJ + t, :])

                def hid_ready(part):
                    def before(t):
                        if part * HJ + t in (0, J - 1):
                            count = J * f + (J - 1 if part == 0 else J)
                            pe.wait_ge(hid_head_made, count)
                            pe.wait_ge(hid_tail_made, count)
                    return before

                with pe.Fori(0, 2 * KD // SLOTS) as i:
                    for s in range(SLOTS):
                        m, part = s // 2, s % 2
                        if part == 0:
                            wait_read(pe, down_place(f, m), i, more=0)
                        product(U_DOWN[f] + s, ps[m], HJ, hid(part), pieces, i, start=part == 0, stop=part == 1,
                                before=hid_ready(part) if m == 0 else None)

            pe.wait_ge(const_made, 1)
            ffn(0, ALL)

            def project(n, pieces, before=None):
                place = MIX_PLACE[n]
                wait_read(pe, place, more=0)
                product(n, ps[place[0]], KD, xg, pieces, before=before)

            def first_projection(t):
                xg_ready(1)(t)
                if t == 6:
                    norm_sum(1, ALL)

            def turn_values():
                wait_read(pe, MIX_PLACE[U_V])
                pe.wait_ge(mixer_const, 2)
                for c in range(1, NC):
                    t0 = N_META + (c - 1) * CHUNK
                    pe.transpose(ps_d[:, c // 4, (c % 4) * P:(c % 4 + 1) * P], v_t[:, t0:t0 + P], ident[:, :])
                pe.transpose(ps_d[0:N_META, 0, 0:P], v_t[:, 0:N_META], ident[:, :]).then_inc(v_turned, 1)

            def scores(c):
                if c == 0:
                    for b in range(2):
                        wait_read(pe, MIX_PLACE[U_Q + 2 + b])
                    pe.wait_ge(k_windows, 1)
                else:
                    pe.wait_ge(exp_made, c)
                w, n = max(c, 1), keys(c)
                for b in range(NB):
                    for g in range(2):
                        rows = slice(64 * g, 64 * g + 64)
                        mm = pe.matmul(ps_c[rows, b // 2, (b % 2) * KEYS:(b % 2) * KEYS + n],
                                       q_t[rows, b, c * CHUNK:(c + 1) * CHUNK], k_win[rows, w, 0:n],
                                       start=True, stop=True)
                mm.then_inc(scores_made, 1)

            def turn_probs(c):
                pe.wait_ge(prob_made, c + 1)
                if c == 0:
                    pe.wait_ge(v_kept, 1)
                else:
                    pe.wait_ge(p_kept, c)
                    pe.wait_ge(ya_kept, c)
                n = keys(c) - N_META
                for b in range(NB):
                    pe.transpose(ps_d[0:n, 0, b * P:(b + 1) * P], prob[:, b, N_META:N_META + n], ident[:, :])
                for b in range(NB):
                    mm = pe.transpose(ps_d[0:N_META, 1, b * P:(b + 1) * P], prob[:, b, 0:N_META], ident[:, :])
                mm.then_inc(p_turned, 1)

            def values(c):
                pe.wait_ge(p_kept, c + 1)
                pe.wait_ge(pm_kept, c + 1)
                n, w = keys(c) - N_META, max(c, 1)
                for g in range(2):
                    rows = slice(64 * g, 64 * g + 64)
                    dst = ps_d[rows, 1, 0:NB * CHUNK]
                    pt = p_t[0:n, :].rearrange("k (b g q) -> k b g q", b=NB, g=2)[:, :, g, :]
                    pm = p_t_meta[:, :].rearrange("k (b g q) -> k b g q", b=NB, g=2)[:, :, g, :]
                    pe.matmul(dst, v_win[0:n, w, rows], pt, start=True, stop=False)
                    mm = pe.matmul(dst, v_meta[:, rows], pm, start=False, stop=True)
                mm.then_inc(pv_made, 1)

            def lru_gate(b, g):
                pe.wait_ge(bd_landed, 64)
                pe.wait_ge(conv_made, b + 1)
                place = MIX_PLACE[g, b]
                wait_read(pe, place, more=0)
                for bank, t0, width in ALL:
                    mm = pe.matmul(ps[place[0]][:, bank, 0:width], gate_bd[:, g, b, :], xc[:, b, t0:t0 + width],
                                   start=True, stop=True)
                mm.then_inc(gates_made, 1)

            project(U_IN, ALL, first_projection)
            for b in range(NB):
                project(U_Q + b, REAL)
            for p in range(NC + 1):
                gates = U_V + p - GATES_IN

                def within(t):
                    if p == 1 and t == 1:
                        turn_values()
                    if p and t == (4 if p == 1 else 2):
                        turn_probs(p - 1)
                    if 0 <= gates < NB and t == 2:
                        lru_gate(gates, 0)
                    if p < NC and t == 3:
                        scores(p)
                    if p and t == (6 if p == 1 else 4 if p == NC else 5):
                        values(p - 1)
                    if 0 <= gates < NB and t == 4:
                        lru_gate(gates, 1)
                project(U_V + p, ALL if U_V + p < U_BRANCH else REAL, within)

            for u in range(2 * NB):
                attn = u < NB
                head, tail = (ya_head, ya_tail) if attn else (yl_head, yl_tail)

                def before(t):
                    if u % NB == 0:
                        pe.wait_ge(ya_head_made if attn else yl_head_made, t % NB + 1)
                        pe.wait_ge(ya_tail_made if attn else yl_tail_made, t % NB + 1)
                    if u == 0 and t == 2:
                        pe.wait_ge(ya_squared, NC)
                        token_sums(sum_sq[:, N_META:L]).then_inc(norm_summed, 1)
                    if u == 1 and t == 4:
                        spread_rstd(0, ps_c[:, 1, :]).then_inc(rstd_spread, 1)
                    if u == 3 and t == 0:
                        pe.wait_ge(lru_summed, 1)
                        token_sums(a_sq[:, 0:SEQ]).then_inc(norm_summed, 1)
                    if u == 3 and t == 6:
                        spread_rstd(1, ps_c[:, 0, :]).then_inc(rstd_spread, 1)
                place = out_place(u)
                wait_read(pe, place, more=0)
                product(U_OUT + u, ps[place[0]], KD, lambda t: (head[:, t % NB, :], tail[:, t % NB, :]),
                        [(0, 0, SEQ)], before=before, group=NB)

            ffn(1, REAL)

            pe.wait_ge(sum_made, 4 * KD - 2)
            token_sums(sum_sq[:, N_META:L], last=False)
            pe.wait_ge(last_square, 1)
            token_sums(last_chunk_sq, first=False).then_inc(norm_summed, 1)
            spread_rstd(2, ps_d[:, 0, :]).then_inc(rstd_spread, 1)
            pe.matmul(ps_d[:, 1, :], ones[:, :], diagonal, start=True, stop=True).then_inc(rstd_spread, 1)

        @block.scalar
        def _(act):
            def split_head(n, i=None):
                cols = unit_tiles(n) * P
                act.wait_ge(w_landed[n % RAW], plus(16 * (n // RAW + 1), i, 16 * SLOTS // RAW))
                if n >= SLOTS:
                    act.wait_ge(units_done, plus(n - SLOTS + 1, i, SLOTS))
                act.activation(w_head[:, n % SLOTS, 0:cols], w_raw[:, n % RAW, 0:cols], ACT.Copy).then_inc(head_made, 1)

            def fetch_table(function):
                act.activation(table_out[:, :], eps[:, 0:1], function)

            def root(which, src, dst, width):
                act.wait_ge(norm_summed, which)
                act.activation(dst, src, ACT.Sqrt, scale=1.0 / width, bias=eps[:, 0:1]).then_inc(rms_made, 1)

            def token_root(which, width):
                root(which, token_sum.rearrange("p (b n) -> p b n", b=TB)[:, :, 0], rms_tok[which], width)

            def ffn(f, pieces):
                cols = span(pieces)

                def four(j, n, i=None):
                    for jj in (j, j + 1):
                        wait_read(act, gu_place(f, 2 * jj), i)
                        act.activation(gate_s[:, cols], gate_s[:, cols], ACT.Silu).then_inc(silu_made, 1)
                        split_head(n + 2 * (jj - j), i)
                        act.wait_ge(hid_made, plus(J * f + jj + 1, i, 2))
                        act.activation(block_of(hid_head, jj, i, 2, cols), up_s[:, cols],
                                       ACT.Copy).then_inc(hid_head_made, 1)
                        split_head(n + 2 * (jj - j) + 1, i)

                root(SUM_FFN1 if f == 0 else SUM_FFN2, banks(ps_c, pieces), by_piece(rstd[:, cols], pieces), D_MODEL)
                with act.Fori(0, TURNS - 1) as i:
                    four(0, U_GU[f] + SLOTS, i)
                four(J - 2, U_DOWN[f])

                def down(m, n, i=None):
                    if n is not None:
                        split_head(n, i)
                    if f == 0:
                        wait_read(act, down_place(f, m), i)
                        gain = vec[:, bass.ds(i * 2 + (VEC["mix"] + m), 1)] if i is not None else col("mix", m)
                        act.activation(block_of(xg_head, m, i, 2), block_of(h, m, i, 2), ACT.Copy,
                                       scale=gain).then_inc(xg_head_made, 1)
                    if n is not None:
                        split_head(n + 1, i)

                with act.Fori(0, 2 * KD // SLOTS - 1) as i:
                    for m in range(2):
                        down(m, U_DOWN[f] + SLOTS + 2 * m, i)
                for m in range(2):
                    down(KD - 2 + m, U_IN + 2 * m if f == 0 else None)

            act.wait_ge(const_made, 1)
            fetch_table(ACT.Sqrt)
            act.wait_ge(vec_landed, 16)
            for k in range(KD):
                act.wait_ge(x_landed[k], 16)
                act.activation(xg_head[:, k, :], h[:, k, :], ACT.Copy, scale=col("ffn1", k)).then_inc(xg_head_made, 1)
                if k == 0:
                    act.wait_ge(half_landed, 16)
                    act.activation(w_head[:, 0, 0:HALF], w_raw[:, 0, 0:HALF], ACT.Copy).then_inc(half_head, 1)
                if k == 1:
                    act.wait_ge(w_landed[0], 16)
                    act.activation(w_head[:, 0, HALF:KD * P], w_raw[:, 0, HALF:KD * P], ACT.Copy).then_inc(head_made, 1)
            split_head(1)
            for k in range(KD):
                if k >= 3:
                    act.wait_ge(sum_made, k - 2)
                dst = sum_sq if k == 0 else (gate_s, up_s)[k % 2]
                act.activation(dst[:, :], h[:, k, :], ACT.Square).then_inc(square_made, 1)
                if k == 3:
                    split_head(2)
            split_head(3)
            ffn(0, ALL)

            root(SUM_MIX, banks(ps_c, ALL), by_piece(rstd[:, :], ALL), D_MODEL)
            for u in range(NB + 1):
                split_head(U_IN + SLOTS + u)
                if u == 1:
                    act.wait_ge(lru_consts, 1)
                    act.activation(small[:, 1, :], small[:, 0, :], ACT.Exp, scale=-1.0).then_inc(lam_exp, 1)

            def keep_turned_values():
                act.wait_ge(v_turned, 1)
                act.activation(v_win[:, 1:NC, :].rearrange("p c d -> p (c d)"),
                               ps_d[:, :, :].rearrange("p a n -> p (a n)")[:, P:NC * P], ACT.Copy)
                act.activation(v_meta[:, :], ps_d[0:N_META, 0, 0:P], ACT.Copy).then_inc(v_kept, 1)

            def exps(c):
                act.wait_ge(bias_made, c + 1)
                if c:
                    act.wait_ge(p_turned, c)
                    act.wait_ge(prob_made, c)
                n = keys(c)
                for b in range(NB):
                    act.activation(prob[:, b, 0:n], ps_c[:, b // 2, (b % 2) * KEYS:(b % 2) * KEYS + n], ACT.Exp,
                                   scale=ATTN_SCALE, bias=small[:, 8, b:b + 1], accum_out=small[:, 9, b:b + 1])
                act.activation(small[:, 11, :], small[:, 10, :], ACT.Exp).then_inc(exp_made, 1)

            def keep_probs(c):
                n = keys(c) - N_META
                act.wait_ge(p_turned, c + 1)
                if c:
                    act.wait_ge(pv_made, c)
                act.activation(p_t[0:n, :], ps_d[0:n, 0, :], ACT.Copy).then_inc(p_kept, 1)

            def keep_gate(b, g):
                act.wait_ge(gates_made, 2 * b + g + 1)
                q = MIX_PLACE[g, b][0]
                act.activation(by_piece((r_a, i_u)[g][:, b, :], ALL), banks(ps[q], ALL),
                               ACT.Copy).then_inc(pair_read[q], 1)

            def gate_sigmoids(b):
                for g, gate in enumerate((r_a, i_u)):
                    wait_read(act, MIX_PLACE[g, b])
                    act.activation(gate[:, b, :], gate[:, b, :], ACT.Sigmoid,
                                   bias=col(("ba", "bx")[g], b)).then_inc(gate_ready, 1)

            def decay(b):
                act.wait_ge(lru_consts, 2)
                act.wait_ge(gate_ready, 2 * b + 1)
                act.activation(one_m_a2[:, b, :], r_a[:, b, :], ACT.Tanh, scale=small[:, 7, b:b + 1])
                act.activation(r_a[:, b, :], r_a[:, b, :], ACT.Exp, scale=small[:, 6, b:b + 1]).then_inc(decay_made, 1)

            for p in range(NC + 1):
                gates = U_V + p - GATES_IN
                if 0 < p < 7:
                    split_head(U_V + p + SLOTS - 1)
                if p == 1:
                    keep_turned_values()
                if p:
                    keep_probs(p - 1)
                if 0 <= gates < NB:
                    keep_gate(gates, 0)
                if p in (5, 7):
                    fetch_table(ACT.Exp)
                if p < NC:
                    exps(p)
                if 0 <= gates < NB:
                    keep_gate(gates, 1)
                if p in (4, 6):
                    gate_sigmoids(p - 4)
                    gate_sigmoids(p - 3)
                if p >= 7:
                    split_head(U_V + p + SLOTS - 1)
                if p in (5, 7):
                    decay(p - 5)
                    decay(p - 4)

            def lru_root(b):
                act.wait_ge(om_made, b + 1)
                act.activation(one_m_a2[:, b, :], one_m_a2[:, b, :], ACT.Sqrt).then_inc(root_made, 1)

            lru_root(0)
            lru_root(1)
            act.wait_ge(ya_kept, NC)
            for b in range(NB):
                act.activation(ya_head[:, b, :], y_attn[:, b, :], ACT.Copy, scale=col("attn", b)).then_inc(ya_head_made, 1)
            lru_root(2)
            lru_root(3)
            token_root(SUM_ATTN, ATTN_WIDTH)
            split_head(U_OUT + NB - 1)
            for b in range(NB):
                wait_read(act, MIX_PLACE[U_BRANCH + b])
                act.activation(gelu[:, b, :], gelu[:, b, :], ACT.Gelu_apprx_tanh).then_inc(gelu_made, 1)
            act.wait_ge(ya_tail_made, NB)
            for b in range(NB):
                for y in (2 * b, 2 * b + 1):
                    if y < NB:
                        act.wait_ge(yl_made, y + 1)
                        yb = r_a[:, y, 0:SEQ]
                        act.activation(yl_head[:, y, :], yb, ACT.Copy, scale=col("lru", y)).then_inc(yl_head_made, 1)
                        act.activation(y_attn[:, y, :] if y else a_sq[:, 0:SEQ], yb, ACT.Square).then_inc(yl_squared, 1)
                if b == 2:
                    fetch_table(ACT.Sqrt)
                    token_root(SUM_LRU, LRU_WIDTH)
                split_head(U_OUT + NB + b)
            for u in range(NB):
                split_head(U_GU[1] + u)
                for k in (2 * u, 2 * u + 1):
                    act.wait_ge(h_ready, k + 1)
                    act.activation(xg_head[:, k, N_META:L], h[:, k, N_META:L], ACT.Copy,
                                   scale=col("ffn2", k)).then_inc(xg_head_made, 1)
            ffn(1, REAL)

            fetch_table(ACT.Sqrt)
            for m in POOL_OUT:
                act.wait_ge(sum_made, 3 * KD + m)
                act.activation(h[:, m, N_META:L], h[:, m, N_META:L], ACT.Copy, scale=col("final", m)).then_inc(gained, 1)
            wait_read(act, down_place(1, KD - 1))
            act.activation(last_chunk_sq, h[:, KD - 1, N_META:L], ACT.Square).then_inc(last_square, 1)
            token_root(SUM_FINAL, D_MODEL)
            act.wait_ge(rstd_spread, 4)
            act.activation(rstd[:, N_META:L], ps_d[:, 1, :], ACT.Copy).then_inc(rstd_kept, 1)

        @block.vector
        def _(dve):
            chained = [0]

            def chain(ins):
                chained[0] += 1
                ins.then_inc(dve_chain, 1)
                dve.wait_ge(dve_chain, chained[0])

            def split_tail(n, i=None):
                cols = unit_tiles(n) * P
                dve.wait_ge(head_made, plus(n + 1, i, SLOTS))
                dve.tensor_tensor(w_tail[:, n % SLOTS, 0:cols], w_raw[:, n % RAW, 0:cols],
                                  w_head[:, n % SLOTS, 0:cols].bitcast(F32), ALU.subtract).then_inc(tail_made, 1)

            def tail_of(dst, src, gain, head):
                return dve.scalar_tensor_tensor(out=dst, in0=src, scalar=gain, in1=head.bitcast(F32),
                                                op0=ALU.mult, op1=ALU.subtract)

            def invert(which, ap):
                dve.wait_ge(rms_made, which)
                dve.reciprocal(ap, ap).then_inc(rstd_made, 1)
                dve.wait_ge(rstd_made, which)

            def scaled(place, dst, pieces):
                q = place[0]
                dve.tensor_tensor(by_piece(dst, pieces), banks(ps[q], pieces),
                                  by_piece(rstd[:, span(pieces)], pieces), ALU.mult).then_inc(pair_read[q], 1)

            def ffn(f, pieces):
                cols = span(pieces)

                def four(j, n, i=None):
                    for jj in (j, j + 1):
                        dve.wait_ge(units_done, plus(U_GU[f] + 2 * jj + 1, i, SLOTS))
                        if jj:
                            dve.wait_ge(hid_made, plus(J * f + jj, i, 2))
                        scaled(gu_place(f, 2 * jj), gate_s[:, cols], pieces)
                        split_tail(n + 2 * (jj - j), i)
                        dve.wait_ge(units_done, plus(U_GU[f] + 2 * jj + 2, i, SLOTS))
                        if jj:
                            dve.wait_ge(hid_tail_made, plus(J * f + jj, i, 2))
                        scaled(gu_place(f, 2 * jj + 1), up_s[:, cols], pieces)
                        split_tail(n + 2 * (jj - j) + 1, i)

                invert(SUM_FFN1 if f == 0 else SUM_FFN2, rstd[:, cols])
                four(0, U_GU[f] + SLOTS)
                with dve.Fori(0, TURNS - 2) as i:
                    four(2, U_GU[f] + 2 * SLOTS, i)
                four(J - 2, U_DOWN[f])

                def down(m, n, i=None):
                    if n is not None:
                        split_tail(n, i)
                    dve.wait_ge(units_done, plus(U_DOWN[f] + 2 * m + 2, i, SLOTS))
                    hm = block_of(h, m, i, 2, cols)
                    dve.scalar_tensor_tensor(out=by_piece(hm, pieces), in0=banks(ps[m % 2], pieces), scalar=0.5,
                                             in1=by_piece(hm, pieces), op0=ALU.mult,
                                             op1=ALU.add).then_inc(pair_read[m % 2], 1)
                    if n is not None:
                        split_tail(n + 1, i)
                    if f == 0:
                        wait_read(dve, down_place(f, m), i)
                        dve.wait_ge(xg_head_made, plus(KD + m + 1, i, 2))
                        gain = vec[:, bass.ds(i * 2 + (VEC["mix"] + m), 1)] if i is not None else col("mix", m)
                        tail_of(block_of(xg_tail, m, i, 2), hm, gain, block_of(xg_head, m, i, 2)).then_inc(xg_tail_made, 1)

                with dve.Fori(0, 2 * KD // SLOTS - 1) as i:
                    for m in range(2):
                        down(m, U_DOWN[f] + SLOTS + 2 * m, i)
                for m in range(2):
                    down(KD - 2 + m, U_IN + 2 * m if f == 0 else None)

            dve.wait_ge(vec_landed, 16)
            for k in range(KD):
                dve.wait_ge(x_landed[k], 16)
                dve.wait_ge(xg_head_made, k + 1)
                tail_of(xg_tail[:, k, :], h[:, k, :], col("ffn1", k), xg_head[:, k, :]).then_inc(xg_tail_made, 1)
                if k < 2:
                    cols = slice(k * HALF, (k + 1) * HALF)
                    dve.wait_ge((half_head, head_made)[k], 1)
                    dve.tensor_tensor(w_tail[:, 0, cols], w_raw[:, 0, cols], w_head[:, 0, cols].bitcast(F32),
                                      ALU.subtract).then_inc((half_tail, tail_made)[k], 1)
            split_tail(1)
            for k in range(1, KD):
                dve.wait_ge(square_made, k + 1)
                dve.tensor_tensor(sum_sq[:, :], sum_sq[:, :], (gate_s, up_s)[k % 2][:, :], ALU.add).then_inc(sum_made, 1)
                dve.wait_ge(sum_made, k)
                if k == 4:
                    split_tail(2)
            split_tail(3)
            ffn(0, ALL)

            def vcols(name):
                return vec[:, VEC[name]:VEC[name] + NB]

            def lru_exponents():
                lam, s = vcols("lam"), small
                chain(dve.tensor_scalar(s[:, 2, :], lam, -1.0, None, ALU.mult))
                dve.tensor_tensor(s[:, 0, :], lam, s[:, 2, :], ALU.max).then_inc(lru_consts, 1)
                dve.wait_ge(lam_exp, 1)
                chain(dve.tensor_scalar(s[:, 2, :], s[:, 1, :], 2.0, None, ALU.add))
                chain(dve.reciprocal(s[:, 3, :], s[:, 2, :]))
                chain(dve.tensor_tensor(s[:, 2, :], s[:, 1, :], s[:, 3, :], ALU.mult))
                chain(dve.tensor_tensor(s[:, 3, :], s[:, 2, :], s[:, 2, :], ALU.mult))
                chain(dve.tensor_scalar(s[:, 4, :], s[:, 3, :], 1.0 / 17.0, None, ALU.mult))
                for n in range(15, 1, -2):
                    chain(dve.scalar_tensor_tensor(out=s[:, 4, :], in0=s[:, 4, :], scalar=1.0 / n, in1=s[:, 3, :],
                                                   op0=ALU.add, op1=ALU.mult))
                chain(dve.scalar_tensor_tensor(out=s[:, 4, :], in0=s[:, 4, :], scalar=1.0, in1=s[:, 2, :],
                                               op0=ALU.add, op1=ALU.mult))
                chain(dve.tensor_scalar(s[:, 5, :], lam, -1.0, 0.0, ALU.mult, ALU.max))
                chain(dve.scalar_tensor_tensor(out=s[:, 5, :], in0=s[:, 4, :], scalar=2.0, in1=s[:, 5, :],
                                               op0=ALU.mult, op1=ALU.add))
                dve.tensor_scalar(s[:, 6, :], s[:, 5, :], -LRU_C, None, ALU.mult)
                dve.tensor_scalar(s[:, 7, :], s[:, 5, :], LRU_C, None, ALU.mult).then_inc(lru_consts, 1)
                chain(dve.tensor_scalar(s[:, 12, :], vcols("sink"), -1.0, None, ALU.mult))

            dve.wait_ge(units_done, U_IN)
            invert(SUM_MIX, rstd[:, :])

            def project(n, dst, pieces):
                dve.wait_ge(units_done, n + 1)
                scaled(MIX_PLACE[n], dst, pieces)

            project(U_IN, k_t[:, :], ALL)
            split_tail(U_IN + SLOTS)
            wait_read(dve, MIX_PLACE[U_IN])
            w = NC - 1
            chunks = k_t[:, N_META:L].rearrange("p (w n) -> p w n", w=NC)
            dve.tensor_copy(k_win[:, 1:NC, N_META:N_META + CHUNK], chunks[:, 0:w, :])
            dve.tensor_copy(k_win[:, 1:NC, N_META + CHUNK:KEYS], chunks[:, 1:NC, :])
            dve.tensor_copy(k_win[:, 1:NC, 0:N_META],
                            k_t[:, 0:N_META].unsqueeze(1).broadcast_to([P, w, N_META])).then_inc(k_windows, 1)
            for b in range(NB):
                project(U_Q + b, q_t[:, b, :], REAL)
                split_tail(U_Q + SLOTS + b)
                if b == 0:
                    lru_exponents()

            def softmax_bias(c):
                dve.wait_ge(scores_made, c + 1)
                chain(dve.tensor_reduce(small[:, 13, :].rearrange("p (a b) -> p a b", a=2),
                                        ps_c[:, :, 0:2 * KEYS].rearrange("p a (b n) -> p a b n", b=2)[:, :, :, 0:keys(c)],
                                        AX_X, ALU.max))
                chain(dve.scalar_tensor_tensor(out=small[:, 8, :], in0=small[:, 13, :], scalar=-ATTN_SCALE,
                                               in1=small[:, 12, :], op0=ALU.mult, op1=ALU.min))
                dve.tensor_tensor(small[:, 10, :], vcols("sink"), small[:, 8, :], ALU.add).then_inc(bias_made, 1)

            def softmax_scale(c):
                n = keys(c)
                dve.wait_ge(exp_made, c + 1)
                chain(dve.tensor_tensor(small[:, 14, :], small[:, 9, :], small[:, 11, :], ALU.add))
                chain(dve.reciprocal(small[:, 15, :], small[:, 14, :]))
                dve.tensor_tensor(prob[:, :, 0:n], prob[:, :, 0:n],
                                  small[:, 15, :].unsqueeze(2).broadcast_to([P, NB, n]),
                                  ALU.mult).then_inc(prob_made, 1)

            def keep_meta_probs(c):
                dve.wait_ge(p_turned, c + 1)
                if c:
                    dve.wait_ge(pv_made, c)
                dve.tensor_copy(p_t_meta[:, :], ps_d[0:N_META, 1, :]).then_inc(pm_kept, 1)

            def keep_values(c):
                dve.wait_ge(pv_made, c + 1)
                dve.tensor_copy(y_attn[:, :, c * CHUNK:(c + 1) * CHUNK],
                                ps_d[:, 1, 0:NB * CHUNK].rearrange("p (b q) -> p b q", b=NB)).then_inc(ya_kept, 1)

            def conv_tap(b, tap):
                last = CONV_WIDTH - 1
                weight = col("conv_w", tap * NB + b)
                if tap == last:
                    wait_read(dve, MIX_PLACE[U_X + b])
                    dve.wait_ge(mixer_const, 3)
                    chain(dve.tensor_scalar(xc[:, b, :], x_pad[:, last:last + L], weight, col("conv_b", b),
                                            ALU.mult, ALU.add))
                    return
                ins = dve.scalar_tensor_tensor(out=xc[:, b, :], in0=x_pad[:, tap:tap + L], scalar=weight,
                                               in1=xc[:, b, :], op0=ALU.mult, op1=ALU.add)
                if tap:
                    chain(ins)
                else:
                    ins.then_inc(conv_made, 1)

            def one_less_a_squared(b):
                dve.wait_ge(a_sq_made, b + 1)
                dve.scalar_tensor_tensor(out=one_m_a2[:, b, :], in0=a_sq[:, :], scalar=1.0,
                                         in1=one_m_a2[:, b, :], op0=ALU.add, op1=ALU.mult).then_inc(om_made, 1)

            def states(b):
                dve.wait_ge(u_made, b + 1)
                chain(dve.tensor_tensor_scan(xc[:, b, :], r_a[:, b, :], i_u[:, b, :], 0.0, ALU.mult, ALU.add))

            for p in range(NC + 1):
                conv = p - 2 if 0 <= p - 2 < NB else None
                if p == 1:
                    project(U_V, v_t[:, :], ALL)
                elif conv is not None:
                    if conv:
                        dve.wait_ge(conv_made, conv)
                    project(U_X + conv, x_pad[:, CONV_WIDTH - 1:], ALL)
                elif p:
                    b = p - 2 - NB
                    project(U_BRANCH + b, gelu[:, b, :], REAL)
                if 0 < p < 7:
                    split_tail(U_V + p + SLOTS - 1)
                if p == 6:
                    one_less_a_squared(0)
                if conv is not None:
                    conv_tap(conv, 3)
                if p > 1:
                    keep_meta_probs(p - 1)
                if p == 6:
                    one_less_a_squared(1)
                if p == 8:
                    split_tail(U_V + p + SLOTS - 1)
                    one_less_a_squared(2)
                if conv is not None:
                    conv_tap(conv, 2)
                if p < NC:
                    softmax_bias(p)
                if p == 1:
                    keep_meta_probs(0)
                if conv is not None:
                    conv_tap(conv, 1)
                    conv_tap(conv, 0)
                if p:
                    keep_values(p - 1)
                if p < NC:
                    softmax_scale(p)
                if p == 7:
                    split_tail(U_V + p + SLOTS - 1)
            for b in range(NB):
                dve.wait_ge(ya_head_made, b + 1)
                tail_of(ya_tail[:, b, :], y_attn[:, b, :], col("attn", b), ya_head[:, b, :]).then_inc(ya_tail_made, 1)
            one_less_a_squared(3)
            project(U_OUT - 1, gelu[:, NB - 1, :], REAL)
            split_tail(U_OUT + NB - 1)

            def token_rstd(which):
                rms = rms_tok[which]
                invert(which, rms)
                for b in range(TB):
                    dve.tensor_scalar(diagonal[:, b * P:(b + 1) * P], ident[:, :], rms[:, b:b + 1], None,
                                      ALU.mult).then_inc(diagonal_made, 1)

            def out_scaled(u, factor, first=0, last=1):
                dve.wait_ge(units_done, U_OUT + u + 1)
                q, n = out_place(u)[0], last + 1 - first
                ins = dve.tensor_tensor(y_scaled[u % 2][:, first:last + 1, :], ps[q][:, first:last + 1, :],
                                        factor.unsqueeze(1).broadcast_to([P, n, SEQ]), ALU.mult)
                if last:
                    ins.then_inc(pair_read[q], 1)
                    wait_read(dve, out_place(u))
                else:
                    chain(ins)

            for b in range(NB):
                states(b)
                if b == 0:
                    token_rstd(SUM_ATTN)
            for b in range(NB):
                dve.wait_ge(gelu_made, b + 1)
                dve.tensor_tensor(r_a[:, b, 0:SEQ], gelu[:, b, :], xc[:, b, N_META:L], ALU.mult).then_inc(yl_made, 1)
            dve.wait_ge(rstd_spread, 1)
            chain(dve.tensor_copy(rstd_attn, ps_c[:, 1, :]))
            for b in range(NB):
                for y in (2 * b, 2 * b + 1):
                    if y < NB:
                        dve.wait_ge(yl_head_made, y + 1)
                        tail_of(yl_tail[:, y, :], r_a[:, y, 0:SEQ], col("lru", y), yl_head[:, y, :]).then_inc(yl_tail_made, 1)
                if b == 2:
                    token_rstd(SUM_LRU)
                if b > 1:
                    dve.wait_ge(h_attn, b - 1)
                out_scaled(b, rstd_attn)
                split_tail(U_OUT + NB + b)
            dve.wait_ge(rstd_spread, 2)
            chain(dve.tensor_copy(rstd_lru, ps_c[:, 0, :]))
            dve.wait_ge(h_attn, NB)
            for u in range(NB):
                if u > 1:
                    dve.wait_ge(h_ready, 2 * (u - 1))
                for first, last in ((0, 1),) if u < NB - 1 else ((0, 0), (1, 1)):
                    out_scaled(NB + u, rstd_lru, first, last)
                    hk = h[:, 2 * u + first:2 * u + last + 1, N_META:L]
                    dve.tensor_tensor(hk, hk, y_scaled[u % 2][:, first:last + 1, :],
                                      ALU.add).then_inc(h_ready, last + 1 - first)
                if u < NB - 1:
                    split_tail(U_GU[1] + u)
                for k in (2 * u, 2 * u + 1):
                    dve.wait_ge(h_ready, k + 1)
                    dve.wait_ge(xg_head_made, 2 * KD + k + 1)
                    tail_of(xg_tail[:, k, N_META:L], h[:, k, N_META:L], col("ffn2", k),
                            xg_head[:, k, N_META:L]).then_inc(xg_tail_made, 1)
            split_tail(U_GU[1] + NB - 1)
            ffn(1, REAL)

            dve.wait_ge(identity_again, 1)
            token_rstd(SUM_FINAL)
            dve.wait_ge(rstd_spread, 3)
            for m in DVE_OUT:
                dve.scalar_tensor_tensor(out=h[:, m, N_META:L], in0=h[:, m, N_META:L], scalar=col("final", m),
                                         in1=ps_d[:, 0, :], op0=ALU.mult, op1=ALU.mult).then_inc(out_made, 1)

        @block.gpsimd
        def _(pool):
            chained = [0]

            def chain(ins):
                chained[0] += 1
                ins.then_inc(pool_chain, 1)
                pool.wait_ge(pool_chain, chained[0])

            def identity(made):
                chain(pool.memset(ident[:, :], 0.0))
                pool.affine_select(out=ident[:, :], in_=ident[:, :], compare_op=ALU.not_equal, fill=1.0, base=0,
                                   pattern=[[-1, P]], channel_multiplier=1).then_inc(made, 1)

            def clear_sum(which):
                pool.wait_ge(norm_summed, which - 1)
                pool.memset(sum_sq[:, :], 0.0).then_inc(sum_zero, 1)
                pool.wait_ge(sum_zero, {SUM_MIX: 1, SUM_FFN2: 2, SUM_FINAL: 3}[which])

            def add_square(v, k, cols, i=None):
                hk = block_of(h, k, i, 2, cols)
                pool.tensor_tensor(square[:, cols], hk, hk, ALU.mult).then_inc(square_made, 1)
                pool.wait_ge(square_made, plus(KD * v + k + 1, i, 2))
                pool.tensor_tensor(sum_sq[:, cols], sum_sq[:, cols], square[:, cols], ALU.add).then_inc(sum_made, 1)
                pool.wait_ge(sum_made, plus(KD * v + k, i, 2))

            def ffn(f, pieces):
                cols = span(pieces)
                with pool.Fori(0, J // 2) as i:
                    for j in range(2):
                        pool.wait_ge(silu_made, plus(J * f + j + 1, i, 2))
                        wait_read(pool, gu_place(f, 2 * j + 1), i)
                        pool.tensor_tensor(up_s[:, cols], gate_s[:, cols], up_s[:, cols], ALU.mult).then_inc(hid_made, 1)
                        pool.wait_ge(hid_head_made, plus(J * f + j + 1, i, 2))
                        pool.tensor_tensor(block_of(hid_tail, j, i, 2, cols), up_s[:, cols],
                                           block_of(hid_head, j, i, 2, cols).bitcast(F32),
                                           ALU.subtract).then_inc(hid_tail_made, 1)
                v = 2 * f + 1
                clear_sum(SUM_MIX if f == 0 else SUM_FINAL)
                with pool.Fori(0, KD // 2 - 1) as i:
                    for m in range(2):
                        wait_read(pool, down_place(f, m), i)
                        add_square(v, m, cols, i)
                for m in range(KD - 2, KD - f):
                    wait_read(pool, down_place(f, m))
                    add_square(v, m, cols)

            pool.memset(ones[:, :], 1.0)
            pool.memset(eps[:, :], EPS).then_inc(const_made, 1)
            ffn(0, ALL)

            pool.wait_ge(units_done, U_IN)
            pool.memset(gate_bd[:, :, :, :], 0.0).then_inc(mixer_const, 1)
            identity(mixer_const)
            pool.memset(x_pad[:, 0:CONV_WIDTH - 1], 0.0).then_inc(mixer_const, 1)

            pool.wait_ge(norm_summed, SUM_MIX)
            for c in range(NC):
                for b in {5: (0, 1), 7: (2, 3)}.get(c, ()):
                    pool.wait_ge(decay_made, b + 1)
                    if b:
                        pool.wait_ge(om_made, b)
                    pool.tensor_tensor(a_sq[:, :], r_a[:, b, :], r_a[:, b, :], ALU.mult).then_inc(a_sq_made, 1)
                for b in {4: (0, 1), 6: (2, 3)}.get(c, ()):
                    pool.wait_ge(gate_ready, 2 * b + 2)
                    pool.wait_ge(conv_made, b + 1)
                    pool.tensor_tensor(i_u[:, b, :], i_u[:, b, :], xc[:, b, :], ALU.mult).then_inc(ix_made, 1)
                t0 = c * CHUNK
                pool.wait_ge(ya_kept, c + 1)
                sq = square[:, 0:NB * CHUNK].rearrange("p (b q) -> p b q", b=NB)
                two = square[:, NB * CHUNK:NB * CHUNK + 2 * CHUNK].rearrange("p (b q) -> p b q", b=2)
                yc = y_attn[:, :, t0:t0 + CHUNK]
                chain(pool.tensor_tensor(sq, yc, yc, ALU.mult))
                chain(pool.tensor_tensor(two, sq[:, 0:2, :], sq[:, 2:4, :], ALU.add))
                pool.tensor_tensor(sum_sq[:, N_META + t0:N_META + t0 + CHUNK], two[:, 0, :], two[:, 1, :],
                                   ALU.add).then_inc(ya_squared, 1)
            for b in range(NB):
                pool.wait_ge(ix_made, b + 1)
                pool.wait_ge(root_made, b + 1)
                pool.tensor_tensor(i_u[:, b, :], i_u[:, b, :], one_m_a2[:, b, :], ALU.mult).then_inc(u_made, 1)
            lru_sum = a_sq[:, 0:SEQ]
            for b in range(1, NB):
                pool.wait_ge(yl_squared, b + 1)
                ins = pool.tensor_tensor(lru_sum, lru_sum, y_attn[:, b, :], ALU.add)
                if b < NB - 1:
                    chain(ins)
                else:
                    ins.then_inc(lru_summed, 1)
            for b in range(NB):
                wait_read(pool, out_place(b))
                pool.tensor_tensor(h[:, 2 * b:2 * b + 2, N_META:L], h[:, 2 * b:2 * b + 2, N_META:L], y_scaled[b % 2],
                                   ALU.add).then_inc(h_attn, 1)
            clear_sum(SUM_FFN2)
            for k in range(KD):
                pool.wait_ge(h_ready, k + 1)
                add_square(2, k, slice(N_META, L))
            ffn(1, REAL)

            pool.wait_ge(units_done, U_DOWN[1] + 2 * KD)
            identity(identity_again)
            pool.wait_ge(rstd_kept, 1)
            for n, m in enumerate(POOL_OUT):
                pool.wait_ge(gained, n + 1)
                pool.tensor_tensor(h[:, m, N_META:L], h[:, m, N_META:L], rstd[:, N_META:L],
                                   ALU.mult).then_inc(pool_out_made, 1)


def kernel(x, meta_tokens, ffn1_norm, ffn1_w_gate, ffn1_w_up, ffn1_w_down, mix_norm, w_in, attn_sinks, conv_w, conv_b,
           lru_wa, lru_ba, lru_wx, lru_bx, lru_lambda, attn_out_norm, lru_out_norm, w_out, ffn2_norm, ffn2_w_gate,
           ffn2_w_up, ffn2_w_down, final_norm):
    import numpy as np

    import concourse.bacc as bacc
    from concourse.bass_utils import run_bass_kernel_spmd

    def tiles(w, rows, cols):
        return np.asarray(w).reshape(rows, P, cols, P).transpose(0, 2, 1, 3)

    def units(t):
        return np.ascontiguousarray(t.transpose(0, 2, 1, 3).reshape(t.shape[0], P, t.shape[1] * P))

    def gate_up(gate, up):
        both = np.stack([tiles(gate[0], KD, J), tiles(up[0], KD, J)])
        return units(both.transpose(2, 0, 1, 3, 4).reshape(2 * J, KD, P, P))

    def down(w):
        t = tiles(w[0], J, KD).reshape(2, HJ, KD, P, P)
        return units(t.transpose(2, 0, 1, 3, 4).reshape(2 * KD, HJ, P, P))

    def columns(a):
        return np.asarray(a).reshape(-1, P).T

    heads = np.arange(ATTN_WIDTH).reshape(2, NB, HEAD_DIM).transpose(1, 0, 2).reshape(-1)
    w = np.asarray(w_in[0])
    q, k, v, x_lru, branch = np.split(w, np.cumsum([ATTN_WIDTH, P, P, LRU_WIDTH]), axis=1)
    w_in_units = units(tiles(np.concatenate([k, q[:, heads], v, x_lru, branch], axis=1), KD, U_OUT - U_IN)
                       .transpose(1, 0, 2, 3))
    w = np.asarray(w_out[0])
    w = np.concatenate([w[0:ATTN_WIDTH][heads], w[ATTN_WIDTH:]])
    t = tiles(w, 2 * NB, KD).reshape(2, NB, KD // 2, 2, P, P)
    w_out_units = units(t.transpose(0, 2, 3, 1, 4, 5).reshape(2 * NB, KD, P, P))

    def gates(a):
        return np.asarray(a[0]).reshape(NB, P, 64).transpose(1, 0, 2)

    sinks = np.repeat(np.asarray(attn_sinks[0]).reshape(2, NB), 64, axis=0)
    vecs = np.concatenate([columns(a) for a in (
        ffn1_norm[0], mix_norm[0], ffn2_norm[0], final_norm, attn_out_norm[0][heads], lru_out_norm[0], conv_w[0],
        conv_b[0], lru_ba[0], lru_bx[0], lru_lambda[0])] + [sinks], axis=1)
    tokens = np.concatenate([np.asarray(meta_tokens), np.asarray(x[0])])
    arrays = {
        "x_t": tokens.T.reshape(KD, P, L),
        "ffn1_gu": gate_up(ffn1_w_gate, ffn1_w_up), "ffn1_down": down(ffn1_w_down),
        "w_in": w_in_units, "w_out": w_out_units,
        "ffn2_gu": gate_up(ffn2_w_gate, ffn2_w_up), "ffn2_down": down(ffn2_w_down),
        "gate_w": np.stack([gates(lru_wa), gates(lru_wx)], axis=1),
        "vecs": vecs,
    }
    arrays = {name: np.ascontiguousarray(a) for name, a in arrays.items()}
    nc = bacc.Bacc("TRN2", target_bir_lowering=False, num_devices=1)
    args = {name: nc.dram_tensor(name, a.shape, mybir.dt.from_np(a.dtype), kind="ExternalInput").ap()
            for name, a in arrays.items()}
    args["out_t"] = nc.dram_tensor("out_t", (KD, P, SEQ), F32, kind="ExternalOutput").ap()
    build_layer(nc, **args)
    r = run_bass_kernel_spmd(nc, [arrays], core_ids=[0])
    out = r.results[0]["out_t"]
    return np.ascontiguousarray(out.reshape(D_MODEL, SEQ).T)[None]
```
